# Optimizing a Trainium2 kernel written in Bass

```python
import math
import jax, jax.numpy as jnp
from jax import lax
import numpy as np

D_MODEL = 1024
BATCH = 1
SEQ = 512
DEPTH = 2
DEC_BATCH = 1
DEC_SEQ = 32
PAST_LEN = 512

CHUNK = 64
N_MIXERS = 2
N_GLA = (DEPTH + 1) // 2
N_DIFF = DEPTH // 2
GLA_HEADS = 4
GLA_DK = D_MODEL // 2 // GLA_HEADS
GLA_DV = D_MODEL // GLA_HEADS
GLA_RANK = 16
GLA_TAU = 16.0
GLA_IN = 2 * GLA_HEADS * GLA_DK + 2 * GLA_HEADS * GLA_DV + GLA_RANK
DIFF_HEADS = D_MODEL // 128
DIFF_HD = 64
DIFF_DV = 2 * DIFF_HD
DIFF_IN = DIFF_HEADS * (4 * DIFF_HD + DIFF_DV)
Q_BLOCK = 128
D_FF = 2816
CONV_W = 3
EPS = 1e-6

kernel_name = 'hybrid_gla_diffattn_convffn_stream_step'

def rms_norm(x, gain):
    xf = x.astype(jnp.float32)
    y = xf * lax.rsqrt(jnp.mean(xf * xf, axis=-1, keepdims=True) + EPS)
    return (y * gain.astype(jnp.float32)).astype(x.dtype)

def adaln(c, w_ada, b_ada):
    m = jnp.einsum('bd,de->be', jax.nn.silu(c), w_ada) + b_ada
    return jnp.split(m, 6, axis=-1)

def modulate(h, shift, scale):
    return h * (1.0 + scale[:, None, :]) + shift[:, None, :]

def gla_chunk_step(S, inp):
    q, k, v, g = inp
    C = q.shape[1]
    b = jnp.cumsum(g, axis=1)
    qe = q * jnp.exp(b)
    ke = k * jnp.exp(-b)
    causal = jnp.tril(jnp.ones((C, C), dtype=bool))
    att = jnp.where(causal, jnp.einsum('bthd,bshd->bhts', qe, ke), 0.0)
    o = jnp.einsum('bthd,bhde->bthe', qe, S) + jnp.einsum('bhts,bshe->bthe', att, v)
    b_last = b[:, -1]
    k_dec = k * jnp.exp(b_last[:, None] - b)
    S_new = jnp.exp(b_last)[..., None] * S + jnp.einsum('bshd,bshe->bhde', k_dec, v)
    return S_new, o

def gla_mixer(h, S0, w_in, w_alpha, b_alpha, norm_g, w_out):
    B, T, _ = h.shape
    nq = GLA_HEADS * GLA_DK
    nv = GLA_HEADS * GLA_DV
    proj = jnp.einsum('btd,de->bte', h, w_in)
    q, k, v, r, a_low = jnp.split(proj, [nq, 2 * nq, 2 * nq + nv, 2 * nq + 2 * nv], axis=-1)
    logit = jnp.einsum('btr,re->bte', a_low, w_alpha) + b_alpha
    g = jax.nn.log_sigmoid(logit.astype(jnp.float32)) / GLA_TAU
    C = min(CHUNK, T)
    n = T // C

    def chunks(a, dh):
        return a.astype(jnp.float32).reshape(B, n, C, GLA_HEADS, dh).swapaxes(0, 1)

    S_fin, o = lax.scan(gla_chunk_step, S0.astype(jnp.float32),
                        (chunks(q * GLA_DK ** -0.5, GLA_DK), chunks(k, GLA_DK),
                         chunks(v, GLA_DV), chunks(g, GLA_DK)))
    o = o.swapaxes(0, 1).reshape(B, T, GLA_HEADS, GLA_DV)
    o = rms_norm(o, norm_g).astype(h.dtype) * jax.nn.silu(r).reshape(B, T, GLA_HEADS, GLA_DV)
    out = jnp.einsum('bthe,hed->btd', o, w_out.reshape(GLA_HEADS, GLA_DV, D_MODEL))
    return out, S_fin.astype(S0.dtype)

def diff_project(h, w_in, q_gain, k_gain):
    B, T, _ = h.shape
    nqk = DIFF_HEADS * 2 * DIFF_HD
    proj = jnp.einsum('btd,de->bte', h, w_in)
    q, k, v = jnp.split(proj, [nqk, 2 * nqk], axis=-1)
    q = rms_norm(q.reshape(B, T, DIFF_HEADS, 2, DIFF_HD), q_gain)
    k = rms_norm(k.reshape(B, T, DIFF_HEADS, 2, DIFF_HD), k_gain)
    v = v.reshape(B, T, DIFF_HEADS, DIFF_DV)
    return q, k, v

def diff_attend(q, k, v, q_offset, lam):
    B, T = q.shape[:2]
    Tk = k.shape[1]
    qb = min(Q_BLOCK, T)
    nb = T // qb
    q_blocks = q.reshape(B, nb, qb, DIFF_HEADS, 2, DIFF_HD).swapaxes(0, 1)
    k_chunk = jnp.arange(Tk) // CHUNK
    scale = DIFF_HD ** -0.5

    def one_block(args):
        q_blk, j = args
        q_pos = q_offset + j * qb + jnp.arange(qb)
        mask = k_chunk[None, :] <= (q_pos // CHUNK)[:, None]
        s = jnp.einsum('bqhcd,bkhcd->bhcqk', q_blk, k).astype(jnp.float32) * scale
        p = jax.nn.softmax(jnp.where(mask, s, -jnp.inf), axis=-1)
        a = p[:, :, 0] - lam * p[:, :, 1]
        return jnp.einsum('bhqk,bkhe->bqhe', a.astype(v.dtype), v)

    o = lax.map(one_block, (q_blocks, jnp.arange(nb)))
    return o.swapaxes(0, 1).reshape(B, T, DIFF_HEADS, DIFF_DV)

def conv_ffn(h, conv_state, w_in, conv_w, conv_b, w_out):
    T = h.shape[1]
    up = jnp.einsum('btd,de->bte', h, w_in)
    padded = jnp.concatenate([conv_state.astype(up.dtype), up], axis=1)
    conv = conv_b + conv_w[0] * padded[:, 0:T]
    for j in range(1, CONV_W):
        conv = conv + conv_w[j] * padded[:, j:j + T]
    u, gate = jnp.split(conv, 2, axis=-1)
    y = jnp.einsum('btf,fd->btd', jax.nn.silu(gate) * u, w_out)
    return y, padded[:, T:]

def setup_inputs(seed: int = 0) -> dict:
    key = jax.random.key(seed)
    ks = jax.random.split(key, 32)
    f32 = jnp.float32

    def nrm(k, shape, scale):
        return jax.random.normal(k, shape, f32) * scale

    nq = GLA_HEADS * GLA_DK
    nv = GLA_HEADS * GLA_DV
    return {
        'x_prompt': nrm(ks[0], (BATCH, SEQ, D_MODEL), 1.0),
        'x_sample': nrm(ks[1], (DEC_BATCH, DEC_SEQ, D_MODEL), 1.0),
        'state_gla': nrm(ks[2], (N_GLA, DEC_BATCH, GLA_HEADS, GLA_DK, GLA_DV), 0.5),
        'cache_diff_k': nrm(ks[3], (N_DIFF, DEC_BATCH, PAST_LEN, DIFF_HEADS, 2, DIFF_HD), 1.0),
        'cache_diff_v': nrm(ks[4], (N_DIFF, DEC_BATCH, PAST_LEN, DIFF_HEADS, DIFF_DV), 1.0),
        'state_ffn_conv': nrm(ks[5], (DEPTH, DEC_BATCH, CONV_W - 1, 2 * D_FF), 0.5),
        'c_prompt': nrm(ks[6], (BATCH, D_MODEL), 1.0),
        'c_sample': nrm(ks[7], (DEC_BATCH, D_MODEL), 1.0),
        'norm_mix': 1.0 + nrm(ks[8], (DEPTH, D_MODEL), 0.01),
        'norm_ffn': 1.0 + nrm(ks[9], (DEPTH, D_MODEL), 0.01),
        'w_ada': nrm(ks[10], (DEPTH, D_MODEL, 6 * D_MODEL), 0.5 * D_MODEL ** -0.5),
        'b_ada': nrm(ks[11], (DEPTH, 6 * D_MODEL), 0.01),
        'gla_w_in': nrm(ks[12], (N_GLA, D_MODEL, GLA_IN), D_MODEL ** -0.5),
        'gla_w_alpha': nrm(ks[13], (N_GLA, GLA_RANK, nq), GLA_RANK ** -0.5),
        'gla_b_alpha': nrm(ks[14], (N_GLA, nq), 0.1),
        'gla_norm': 1.0 + nrm(ks[15], (N_GLA, GLA_DV), 0.01),
        'gla_w_out': nrm(ks[16], (N_GLA, nv, D_MODEL), nv ** -0.5),
        'diff_w_in': nrm(ks[17], (N_DIFF, D_MODEL, DIFF_IN), D_MODEL ** -0.5),
        'diff_q_norm': 1.0 + nrm(ks[18], (N_DIFF, DIFF_HD), 0.01),
        'diff_k_norm': 1.0 + nrm(ks[19], (N_DIFF, DIFF_HD), 0.01),
        'diff_lambda': nrm(ks[20], (N_DIFF, 4, DIFF_HD), 0.1),
        'diff_norm': 1.0 + nrm(ks[21], (N_DIFF, DIFF_DV), 0.01),
        'diff_w_out': nrm(ks[22], (N_DIFF, DIFF_HEADS * DIFF_DV, D_MODEL), (DIFF_HEADS * DIFF_DV) ** -0.5),
        'ffn_w_in': nrm(ks[23], (DEPTH, D_MODEL, 2 * D_FF), D_MODEL ** -0.5),
        'ffn_conv_w': nrm(ks[24], (DEPTH, CONV_W, 2 * D_FF), CONV_W ** -0.5),
        'ffn_conv_b': nrm(ks[25], (DEPTH, 2 * D_FF), 0.01),
        'ffn_w_out': nrm(ks[26], (DEPTH, D_FF, D_MODEL), D_FF ** -0.5),
    }

def reference(x_prompt, x_sample, state_gla, cache_diff_k, cache_diff_v, state_ffn_conv,
              c_prompt, c_sample, norm_mix, norm_ffn, w_ada, b_ada,
              gla_w_in, gla_w_alpha, gla_b_alpha, gla_norm, gla_w_out,
              diff_w_in, diff_q_norm, diff_k_norm, diff_lambda, diff_norm, diff_w_out,
              ffn_w_in, ffn_conv_w, ffn_conv_b, ffn_w_out):
    xs = [x_prompt, x_sample]
    cs = [c_prompt, c_sample]
    new_gla = [[], []]
    new_k = [[], []]
    new_v = [[], []]
    new_conv = [[], []]
    for i in range(DEPTH):
        j = i // N_MIXERS
        lam_init = 0.8 - 0.6 * math.exp(-0.3 * i)
        for grp in range(2):
            x = xs[grp]
            B = x.shape[0]
            sh1, sc1, gt1, sh2, sc2, gt2 = adaln(cs[grp], w_ada[i], b_ada[i])
            h = modulate(rms_norm(x, norm_mix[i]), sh1, sc1)
            if i % N_MIXERS == 0:
                S0 = jnp.zeros((B, GLA_HEADS, GLA_DK, GLA_DV), x.dtype) if grp == 0 else state_gla[j]
                mix, S_fin = gla_mixer(h, S0, gla_w_in[j], gla_w_alpha[j], gla_b_alpha[j],
                                       gla_norm[j], gla_w_out[j])
                new_gla[grp].append(S_fin)
            else:
                q, k, v = diff_project(h, diff_w_in[j], diff_q_norm[j], diff_k_norm[j])
                lq1, lk1, lq2, lk2 = diff_lambda[j].astype(jnp.float32)
                lam = jnp.exp(jnp.sum(lq1 * lk1)) - jnp.exp(jnp.sum(lq2 * lk2)) + lam_init
                if grp == 0:
                    o = diff_attend(q, k, v, 0, lam)
                else:
                    k_all = jnp.concatenate([cache_diff_k[j].astype(k.dtype), k], axis=1)
                    v_all = jnp.concatenate([cache_diff_v[j].astype(v.dtype), v], axis=1)
                    o = diff_attend(q, k_all, v_all, PAST_LEN, lam)
                o = rms_norm(o, diff_norm[j]) * (1.0 - lam_init)
                mix = jnp.einsum('bthe,hed->btd', o, diff_w_out[j].reshape(DIFF_HEADS, DIFF_DV, D_MODEL))
                new_k[grp].append(k)
                new_v[grp].append(v)
            x = x + gt1[:, None, :] * mix
            h = modulate(rms_norm(x, norm_ffn[i]), sh2, sc2)
            cst = jnp.zeros((B, CONV_W - 1, 2 * D_FF), x.dtype) if grp == 0 else state_ffn_conv[i]
            f, cst_new = conv_ffn(h, cst, ffn_w_in[i], ffn_conv_w[i], ffn_conv_b[i], ffn_w_out[i])
            new_conv[grp].append(cst_new)
            xs[grp] = x + gt2[:, None, :] * f
    y_prompt = xs[0]
    y_sample = xs[1]
    new_state_gla_prompt = jnp.stack(new_gla[0])
    new_state_gla_sample = jnp.stack(new_gla[1])
    new_k_prompt = jnp.stack(new_k[0])
    new_k_sample = jnp.stack(new_k[1])
    new_v_prompt = jnp.stack(new_v[0])
    new_v_sample = jnp.stack(new_v[1])
    new_conv_prompt = jnp.stack(new_conv[0])
    new_conv_sample = jnp.stack(new_conv[1])
    return (y_prompt, y_sample, new_state_gla_prompt, new_state_gla_sample,
            new_k_prompt, new_k_sample, new_v_prompt, new_v_sample,
            new_conv_prompt, new_conv_sample)


_drawn_inputs = setup_inputs


def setup_inputs(seed=0):
    import zlib

    import numpy as np

    out = dict(_drawn_inputs(seed))
    spreads = {}
    factors = {'norm_mix': 4.426,
     'norm_ffn': 5.637,
     'gla_norm': 8.0,
     'diff_q_norm': 38.81,
     'diff_k_norm': 22.452,
     'diff_norm': 64.0,
     'ffn_conv_b': 8.0,
     'cache_diff_k': 8.0,
     'cache_diff_v': 8.0,
     'state_ffn_conv': 3.705,
     'diff_lambda': 3.618}
    for name, (base, spread) in spreads.items():
        noise = np.random.default_rng([zlib.crc32(name.encode()), seed]).standard_normal(out[name].shape)
        drawn = base * np.exp(spread * noise) if base else spread * noise
        out[name] = __import__('jax').numpy.asarray(drawn.astype(out[name].dtype))
    for name, factor in factors.items():
        out[name] = (out[name] * factor).astype(out[name].dtype)
    return out
```

```python
import math
from contextlib import ExitStack

import concourse.bass as bass
from concourse import mybir

F32 = mybir.dt.float32
F32R = mybir.dt.float32r
BF16 = mybir.dt.bfloat16
U32 = mybir.dt.uint32
ALU = mybir.AluOpType
ACT = mybir.ActivationFunctionType
AX_X = mybir.AxisListType.X

P = 128
EPS = 1e-6
TAU = 16.0
CHUNK = 64
BLOCK_COLS = 256


class Steps:

    def __init__(self, eng, sem):
        self.eng, self.sem, self.n, self.at = eng, sem, 0, 0

    def then(self, ins):
        self.n += 1
        ins.then_inc(self.sem, 1)
        self.eng.wait_ge(self.sem, self.at + self.n)

    def loop(self, i, per):
        self.base, self.per, self.start = self.at + self.n, per, self.n
        self.at, self.n = i * per + self.base, 0

    def end(self, count):
        assert self.n == self.per, (self.n, self.per)
        self.at, self.n = self.base + self.per * count, 0


def hybrid_stream_step(nc, A, O):
    D = A["x_prompt"].shape[2]
    TP, TS = A["x_prompt"].shape[1], A["x_sample"].shape[1]
    T = TP + TS
    KT = D // P
    RT = [(r * P, P) for r in range(TP // P)] + [(TP, TS)]
    NR = len(RT)
    NPR = TP // P
    HALF = T // 2
    PB = TP - HALF
    GH, DK, DV = A["state_gla"].shape[2:]
    RANK = A["gla_w_alpha"].shape[1]
    NQ, NV = GH * DK, GH * DV
    DEPTH, _, FF2 = A["ffn_w_in"].shape
    FF = FF2 // 2
    FT = FF // P
    PAST = A["cache_diff_k"].shape[2]
    NPAST = PAST // P
    DH, _, HD = A["cache_diff_k"].shape[3:]
    EV = 2 * HD
    SCALE = HD ** -0.5
    LAM_INIT = 0.8 - 0.6 * math.exp(-0.3)
    W = T + 2
    CH = [6, 6, 6, FT - 18]
    CMAX = max(CH)
    WB = KT * BLOCK_COLS
    ADA_TILES = 6 * KT
    assert T % 4 == 0 and DK == P and EV == P and sum(CH) == FT and all(c % 2 == 0 for c in CH)

    order = [("ada0", 8), ("qk", 4), ("v", 4), ("r", 4), ("gout", 4)]
    ffn_order = [("up", 0), ("up", 1), ("down", 0), ("up", 2), ("down", 1), ("up", 3), ("down", 2), ("down", 3)]
    nblk = lambda kind, c: CH[c] if kind == "up" else D // BLOCK_COLS
    order += [((0, k, c), nblk(k, c)) for k, c in ffn_order]
    order += [("dq", 4), ("dk", 4), ("dv", 4), ("dout", 4)]
    order += [((1, k, c), nblk(k, c)) for k, c in ffn_order]
    BASE, n = {}, 0
    for name, k in order:
        BASE[name] = n
        n += k
    NBLOCKS = n
    ride, n = {}, 0
    RIDES = ["qk", "v", "r", "gout", (0, "up", 0), (0, "up", 1), (0, "up", 3), "dq", "dk"]
    for name in RIDES:
        ride[name] = n
        n += dict(order)[name]
    assert n == 2 * ADA_TILES // 2 - 8
    TILE, n = {}, 0
    tiles = [("norm0", 1), ("qk", 8), ("alow", 1), ("gout", 8), ("norm1", 1)]
    ffn_tiles = lambda l: [((l, k, c), 2 * nblk(k, c)) for k, c in ffn_order]
    tiles += ffn_tiles(0) + [("norm2", 1), ("dout", 8), ("norm3", 1)] + ffn_tiles(1)
    for name, k in tiles:
        TILE[name] = n
        n += k
    READ_BY_ACT = {n for n, _ in tiles if n in ("qk", "alow") or n[:4] == "norm" or "up" in n}
    READ_A, READ_D, FIRST, a, dd, ff = {}, {}, {}, 1, 2, 0
    for name, k in tiles + [("end", 0)]:
        READ_A[name], READ_D[name], FIRST[name] = a, dd, ff
        if name in READ_BY_ACT:
            a += k
        else:
            dd += k
        ff += max(1, k // 2)
    ROWS, n = {}, 0
    for name in ["v", "r", "dq", "dk", "dv"]:
        ROWS[name] = n
        n += 4 * NR
    FIRST_ROWS = {name: k * (NR - 1) // NR for name, k in ROWS.items()}

    ctx = ExitStack()
    with ctx:
        def sb(name, shape, dt=F32, c=ctx):
            return c.enter_context(nc.sbuf_tensor(name, shape, dt))

        def sem(name):
            return ctx.enter_context(nc.semaphore(name))

        ps = ctx.enter_context(nc.psum_tensor("ps", [P, 8, 512], F32))
        bank = lambda b: ps[:, b, :]

        xT = sb("xT", [P, KT, T])
        h_hi = sb("h_hi", [P, KT, T], F32R)
        h_lo = sb("h_lo", [P, KT, T], F32R)
        w_raw = sb("w_raw", [P, 2, WB])
        w_hi = sb("w_hi", [P, 2, WB], F32R)
        w_lo = sb("w_lo", [P, 2, WB], F32R)
        a_raw = sb("a_raw", [P, WB // 2])
        a_hi = sb("a_hi", [P, WB // 2], F32R)
        a_lo = sb("a_lo", [P, WB // 2], F32R)
        ident = sb("ident", [P, P])
        ones = sb("ones", [P, P])
        cum = sb("cum", [P, P])
        low_rows = sb("low_rows", [1, P], BF16)
        neg_cols = sb("neg_cols", [1, P], BF16)
        eps = sb("eps", [P, 1])
        zero2 = sb("zero2", [P, 2])
        norm_g = sb("norm_g", [P, 4, KT])
        b_ada = sb("b_ada", [P, DEPTH, ADA_TILES])
        conv_c = sb("conv_c", [P, 6 * DEPTH, 2 * FT])
        ada = sb("ada", [P, DEPTH, ADA_TILES, 2])
        cs = sb("cs", [P, 2 * KT])
        c_st = sb("c_st", [P, KT, 32], F32R)
        ada_t = sb("ada_t", [32, BLOCK_COLS])
        gain = sb("gain", [P, KT, 2])
        shift = sb("shift", [P, KT, 2])
        gate = sb("gate", [P, KT, 2])
        new_conv = sb("new_conv", [P, 2 * FT, 4])
        stat = sb("stat", [P, 64])
        nc_rows = sb("nc_rows", [2 * FT, 4, P])

        pro = ExitStack()
        x_rows = sb("x_rows", [P, NR, D], c=pro)
        vec_rows = sb("vec_rows", [P, 3 + 6 * DEPTH, P], c=pro)
        pro.close()
        nrm = ExitStack()
        sq = sb("sq", [P, 2, T], c=nrm)
        rstd = sb("rstd", [P, T], c=nrm)
        nrm.close()
        g = ExitStack()
        qk = sb("qk", [P, 2 * GH, T], c=g)
        v_r = sb("v_r", [P, NR, NV], c=g)
        r_r = sb("r_r", [P, NR, NV], c=g)
        alT = sb("alT", [RANK + 1, T], c=g)
        w_alpha = sb("w_alpha", [RANK + 1, NQ], c=g)
        gla_g = sb("gla_g", [P, DV], c=g)
        tA = sb("tA", [P, NQ], c=g)
        tB = sb("tB", [P, NQ], c=g)
        tC = sb("tC", [P, NQ], c=g)
        qe = sb("qe", [P, NQ], c=g)
        kd_r = sb("kd_r", [P, NQ], c=g)
        att = sb("att", [P, NQ], c=g)
        g2 = ExitStack()
        aw = sb("aw", [P, KT, RANK], c=g2)
        aw_hi = sb("aw_hi", [P, KT, RANK], F32R, c=g2)
        aw_lo = sb("aw_lo", [P, KT, RANK], F32R, c=g2)
        g2.close()
        S = sb("S", [P, 3, GH, DV], c=g)
        dec = sb("dec", [P, GH, 2], c=g)
        g.close()
        f = ExitStack()
        act_hi = sb("act_hi", [P, 2, CMAX, W], F32R, c=f)
        act_lo = sb("act_lo", [P, 2, CMAX, W], F32R, c=f)
        up = sb("up", [P, 2, W + 2], c=f)
        cv1 = sb("cv1", [P, 2, W], c=f)
        cv = sb("cv", [P, 2, 2, W], c=f)
        f.close()
        d = ExitStack()
        q_r = sb("q_r", [P, NR, D], c=d)
        k_r = sb("k_r", [P, NR, D], c=d)
        vd_r = sb("vd_r", [P, NR, D], c=d)
        d2 = ExitStack()
        ssq = sb("ssq", [P, 2 * BLOCK_COLS], c=d2)
        lam_in = sb("lam_in", [P, 4, HD], c=d2)
        d2.close()
        qn = sb("qn", [P, NR, EV], c=d)
        kn = sb("kn", [P, NR, EV], c=d)
        kc, vc = (a_raw[:, n:n + PAST].rearrange("p (r e) -> p r e", e=EV) for n in (0, PAST))
        qT = sb("qT", [P, T], c=d)
        kT = sb("kT", [P, T], c=d)
        kcT = sb("kcT", [P, PAST], c=d)
        pr = sb("pr", [P, 2, 2, PAST + TS], c=d)
        aT = sb("aT", [P, PAST], c=d)
        q_gain = sb("q_gain", [P, HD], c=d)
        k_gain = sb("k_gain", [P, HD], c=d)
        d_gain = sb("d_gain", [P, EV], c=d)
        ss = sb("ss", [P, NR, 2, 2 * DH], c=d)
        rs = sb("rs", [P, NR, 2, 2 * DH], c=d)
        osq = sb("osq", [P, EV], c=d)
        vs = sb("vs", [P, EV], c=d)
        oss = sb("oss", [P, NR, DH], c=d)
        ors = sb("ors", [P, NR, DH], c=d)
        d.close()
        e = ExitStack()
        y_rows = sb("y_rows", [P, 2, D], c=e)
        e.close()

        const_in = sem("const_in")
        vec_in = sem("vec_in")
        consts = sem("consts")
        ident_zero = sem("ident_zero")
        w_in = [sem("w_in0"), sem("w_in1")]
        w_hi_ok = sem("w_hi_ok")
        w_lo_ok = sem("w_lo_ok")
        w_used = sem("w_used")
        a_in = sem("a_in")
        a_hi_ok = sem("a_hi_ok")
        a_lo_ok = sem("a_lo_ok")
        a_used = sem("a_used")
        ada_done = sem("ada_done")
        ada_free = sem("ada_free")
        tile_done = sem("tile_done")
        tile_read_a = sem("tile_read_a")
        tile_read_d = sem("tile_read_d")
        rows_done = sem("rows_done")
        rows_free = sem("rows_free")
        dve_step = sem("dve_step")
        act_step = sem("act_step")
        turned = sem("turned")
        turned_out = sem("turned_out")
        c_hi_ok = sem("c_hi_ok")
        c_st_ok = sem("c_st_ok")
        x_loaded = sem("x_loaded")
        sq_ok = sem("sq_ok")
        sq_used = sem("sq_used")
        rms_used = sem("rms_used")
        xs_ok = sem("xs_ok")
        h_hi_ok = sem("h_hi_ok")
        h_ok = sem("h_ok")
        mod_ok = sem("mod_ok")
        up_ok = sem("up_ok")
        conv_ok = sem("conv_ok")
        silu_ok = sem("silu_ok")
        prod_ok = sem("prod_ok")
        act_hi_ok = sem("act_hi_ok")
        act_ok = sem("act_ok")
        state_out = sem("state_out")
        v_out = sem("v_out")
        phase_in = sem("phase_in")

        L = {}
        for name in ["al_ok", "aw_hi_ok", "aw_ok", "logit_ok", "logit_out", "g_ok", "b_ok", "b_sb_ok", "bd_ok", "exp_ok", "qe_ok",
                     "kd_turned", "kd_out", "attn_ok", "attn_out", "u_ok", "s1_ok", "s2_ok", "o_ok", "oss_ok", "on_ok",
                     "on_turned", "on_hi", "on_lo", "s_zero",
                     "ssq_ok", "ssq_used", "qkv_ok", "rs_ok", "qn_ok", "qn_gained", "heads_turned", "heads_outA", "heads_outD",
                     "sc_ok", "mx_ok", "p_ok", "a_ok", "a_turned", "a_out", "av_ok", "av_out", "osq_ok", "kc_in", "kc_in2",
                     "kn_out", "on2_ok", "on3_ok", "fin_turned", "fin_out", "fin_stored0", "fin_stored1", "nc_turned", "nc_out", "nc_stored",
                     "lam_ok", "lsp_ok", "oss_raw", "s_in", "dg_ok", "vs_ok"]:
            L[name] = sem(name)

        ada_w = A["w_ada"].rearrange("l (k p) e -> l p k e", p=P)
        gla_w = A["gla_w_in"][0].rearrange("(k p) e -> p k e", p=P)
        gla_o = A["gla_w_out"][0].rearrange("(k p) e -> p k e", p=P)
        dif_w = A["diff_w_in"][0].rearrange("(k p) e -> p k e", p=P)
        dif_o = A["diff_w_out"][0].rearrange("(k p) e -> p k e", p=P)
        ffn_i = A["ffn_w_in"].rearrange("l (k p) e -> l p k e", p=P)
        ffn_o = A["ffn_w_out"].rearrange("l (k p) e -> l p k e", p=P)
        blk = lambda t, s, kt=KT: t[:, s, 0:kt * BLOCK_COLS].rearrange("p (k c) -> p k c", k=kt)
        ablk = lambda t: t[:, :].rearrange("p (k c) -> p k c", k=KT // 2)
        slot = lambda t, h, n=HALF, m=P: ps[0:m, 2 * (t % 2) + h, 0:n]

        def shared_ride(name, l=None):
            r = ride.get(name)
            if r is None:
                return None
            return (0, r + 8) if r < ADA_TILES // 2 - 8 else (1, r - (ADA_TILES // 2 - 8))

        block = ctx.enter_context(nc.Block())

        @block.sync
        def _(sp):
            sp.dma_start(x_rows[:, 0:NPR, :], A["x_prompt"][0].rearrange("(r p) d -> p r d", p=P)).then_inc(const_in, 16)
            sp.dma_start(x_rows[0:TS, NPR, :], A["x_sample"][0]).then_inc(const_in, 16)
            tiled = lambda ap: ap.rearrange("(k p) -> k p", p=P)
            sp.dma_start(vec_rows[0:KT, 0, :], tiled(A["c_prompt"][0])).then_inc(vec_in, 16)
            sp.dma_start(vec_rows[KT:2 * KT, 0, :], tiled(A["c_sample"][0])).then_inc(vec_in, 16)
            sp.dma_start(vec_rows[0:2 * KT, 1, :], A["norm_mix"].rearrange("l (k p) -> (l k) p", p=P)).then_inc(vec_in, 16)
            sp.dma_start(vec_rows[2 * KT:4 * KT, 1, :], A["norm_ffn"].rearrange("l (k p) -> (l k) p", p=P)).then_inc(vec_in, 16)
            sp.dma_start(vec_rows[0:DEPTH * ADA_TILES, 2, :], A["b_ada"].rearrange("l (k p) -> (l k) p", p=P)).then_inc(vec_in, 16)
            for l in range(DEPTH):
                sp.dma_start(vec_rows[0:2 * FT, 3 + 6 * l:6 + 6 * l, :],
                             A["ffn_conv_w"][l].rearrange("j (k p) -> k j p", p=P)).then_inc(vec_in, 16)
                sp.dma_start(vec_rows[0:2 * FT, 6 + 6 * l, :], tiled(A["ffn_conv_b"][l])).then_inc(vec_in, 16)
                sp.dma_start(vec_rows[0:2 * FT, 7 + 6 * l:9 + 6 * l, :],
                             A["state_ffn_conv"][l, 0].rearrange("j (k p) -> k j p", p=P)).then_inc(vec_in, 16)

            def load(n0, i, src, kt=KT):
                for j in range(2):
                    n = n0 + 2 * i + j
                    if not (isinstance(i, int) and n < 2):
                        sp.wait_ge(w_lo_ok, n - 1)
                    sp.dma_start(blk(w_raw, j, kt), src(i, j)).then_inc(w_in[j], 16)

            def phase(name, src, kt=KT, peel=False):
                pairs = dict(order)[name] // 2
                if peel:
                    load(BASE[name], 0, src, kt)
                with sp.Fori(1 if peel else 0, pairs) as i:
                    load(BASE[name], i, src, kt)

            col = lambda w, c0: (lambda i, j: w[:, :, bass.ds(c0 + (2 * i + j) * BLOCK_COLS, BLOCK_COLS)])

            phase("ada0", col(ada_w[0], 0), peel=True)
            phase("qk", col(gla_w, 0))
            sp.wait_ge(x_loaded, KT - 1)
            sp.dma_start(aw[:, :, :], gla_w[:, :, 2 * NQ + 2 * NV:2 * NQ + 2 * NV + RANK]).then_inc(phase_in, 16)
            sp.dma_start(w_alpha[0:RANK, :], A["gla_w_alpha"][0]).then_inc(phase_in, 16)
            sp.dma_start(w_alpha[RANK:RANK + 1, :], A["gla_b_alpha"]).then_inc(phase_in, 16)
            sp.dma_start(gla_g[:, :], A["gla_norm"][0].partition_broadcast(P)).then_inc(phase_in, 16)
            phase("v", col(gla_w, 2 * NQ))
            phase("r", col(gla_w, 2 * NQ + NV))
            phase("gout", col(gla_o, 0))

            def ffn_loads(l):
                for kind, c in ffn_order:
                    c0 = sum(CH[:c])
                    if kind == "up":
                        phase((l, kind, c), lambda i, j, c0=c0: ffn_i[l][:, :, bass.ds(j * FF + (c0 + 2 * i) * P, BLOCK_COLS)])
                    else:
                        phase((l, kind, c), col(ffn_o[l][:, c0:c0 + CH[c], :], 0), kt=CH[c])

            ffn_loads(0)
            sp.wait_ge(w_used, BASE["dq"])
            bc = lambda ap: ap.partition_broadcast(P)
            sp.dma_start(q_gain[:, :], bc(A["diff_q_norm"][0])).then_inc(phase_in, 16)
            sp.dma_start(k_gain[:, :], bc(A["diff_k_norm"][0])).then_inc(phase_in, 16)
            sp.dma_start(d_gain[:, :], bc(A["diff_norm"][0])).then_inc(phase_in, 16)
            sp.dma_start(lam_in[:, :, :], bc(A["diff_lambda"][0])).then_inc(phase_in, 16)
            phase("dq", col(dif_w, 0))
            phase("dk", col(dif_w, D))
            phase("dv", col(dif_w, 2 * D))
            load(BASE["dout"], 0, col(dif_o, 0))
            sp.wait_ge(rows_free, ROWS["dv"] + 4 * NR + 2)
            ov = [O[6][0, 0].rearrange("t h e -> t (h e)"), O[7][0, 0].rearrange("t h e -> t (h e)")]
            sp.dma_start(ov[0].rearrange("(r p) e -> p r e", p=P), vd_r[:, 0:NPR, :]).then_inc(v_out, 16)
            sp.dma_start(ov[1], vd_r[0:TS, NPR, :]).then_inc(v_out, 16)
            ck = A["cache_diff_k"][0, 0].rearrange("(r p) h s d -> p r (h s d)", p=P)
            cvv = A["cache_diff_v"][0, 0].rearrange("(r p) h e -> p r (h e)", p=P)
            ok0 = O[4][0, 0].rearrange("(r p) h s d -> p r (h s d)", p=P)
            ok1 = O[5][0, 0].rearrange("t h s d -> t (h s d)")
            sp.wait_ge(a_lo_ok, 4 * (ADA_TILES // 2) - 16)
            sp.sem_inc(L["kn_out"], 1)
            with sp.Fori(0, DH) as h:
                sp.wait_ge(L["heads_turned"], h + 1)
                sp.dma_start(kc[:, :, :], ck[:, :, bass.ds(h * EV, EV)]).then_inc(L["kc_in"], 16)
                sp.wait_ge(L["av_ok"], h * NR + 1)
                sp.dma_start(vc[:, :, :], cvv[:, :, bass.ds(h * EV, EV)]).then_inc(L["kc_in2"], 16)
                sp.wait_ge(L["qn_gained"], h + 1)
                sp.dma_start(ok0[:, :, bass.ds(h * EV, EV)], kn[:, 0:NPR, :]).then_inc(L["kn_out"], 16)
                sp.dma_start(ok1[:, bass.ds(h * EV, EV)], kn[0:TS, NPR, :]).then_inc(L["kn_out"], 16)
            load(BASE["dout"], 1, col(dif_o, 0))
            ffn_loads(1)

            for r, (c0, m) in enumerate(RT):
                sp.wait_ge(L["fin_out"], r + 1)
                dst = O[0][0, c0:c0 + m, :] if r < NPR else O[1][0]
                sp.dma_start(dst, y_rows[0:m, r % 2, :]).then_inc(L["fin_stored%d" % (r % 2)], 16)
            sp.wait_ge(L["fin_stored0"], 16 * ((NR + 1) // 2))
            sp.wait_ge(L["fin_stored1"], 16 * (NR // 2))
            sp.wait_ge(L["kn_out"], 32 * DH + 1)
            sp.wait_ge(L["nc_stored"], 64 * DEPTH)
            sp.wait_ge(v_out, 32)
            sp.wait_ge(state_out, 32)

        @block.gpsimd
        def _(pool):
            pool.memset(ident[:, :], 0.0).then_inc(ident_zero, 1)
            pool.memset(ones[:, :], 1.0).then_inc(ident_zero, 1)
            pool.memset(cum[:, :], 0.0).then_inc(ident_zero, 1)
            pool.memset(low_rows[:, :], 0.0).then_inc(ident_zero, 1)
            pool.memset(neg_cols[:, :], 0.0).then_inc(ident_zero, 1)
            pool.wait_ge(ident_zero, 5)
            pool.affine_select(out=ident[:, :], in_=ident[:, :], compare_op=ALU.not_equal, fill=1.0, base=0,
                               pattern=[[-1, P]], channel_multiplier=1).then_inc(consts, 1)
            pool.memset(eps[:, :], EPS).then_inc(consts, 1)
            pool.memset(zero2[:, :], 0.0).then_inc(consts, 1)
            pool.memset(low_rows[:, 0:CHUNK], 1.0).then_inc(consts, 1)
            pool.memset(neg_cols[:, CHUNK:P], -1e30).then_inc(consts, 1)
            for c in range(P // CHUNK):
                s = slice(c * CHUNK, (c + 1) * CHUNK)
                pool.memset(cum[s, s], 1.0 / TAU).then_inc(ident_zero, 1)
                pool.wait_ge(ident_zero, 6 + c)
                pool.affine_select(out=cum[s, s], in_=cum[s, s], compare_op=ALU.is_ge, fill=0.0, base=0,
                                   pattern=[[1, CHUNK]], channel_multiplier=-1).then_inc(consts, 1)
            def ada_loads(name):
                l, b0 = shared_ride(name)

                def pair(i):
                    for j in range(2):
                        for half in range(2):
                            a = 2 * (ride[name] + 2 * i + j) + half
                            if not (isinstance(i, int) and a < 1):
                                pool.wait_ge(a_lo_ok, a)
                            pool.dma_start(ablk(a_raw), ada_w[l][:, half * KT // 2:(half + 1) * KT // 2,
                                                                 bass.ds((b0 + 2 * i + j) * BLOCK_COLS, BLOCK_COLS)]).then_inc(a_in, 16)

                if ride[name] == 0:
                    pair(0)
                with pool.Fori(1 if ride[name] == 0 else 0, dict(order)[name] // 2) as i:
                    pair(i)

            for name in ("qk", "v", "r"):
                ada_loads(name)
            pool.wait_ge(L["o_ok"], NPR)
            pool.dma_start(S[:, (2 * NPR + 1) % 3], A["state_gla"][0, 0].rearrange("h d e -> d h e")).then_inc(L["s_in"], 16)
            pool.wait_ge(L["s2_ok"], NPR)
            pool.dma_start(O[2][0, 0].rearrange("h d e -> d h e"), S[:, (2 * NPR) % 3]).then_inc(state_out, 16)
            pool.wait_ge(L["s2_ok"], NPR + 1)
            pool.dma_start(O[3][0, 0].rearrange("h d e -> d h e"), S[:, (2 * NPR + 2) % 3]).then_inc(state_out, 16)
            for name in RIDES[3:]:
                ada_loads(name)
            grp = lambda t: t[:, :, :].rearrange("p r (s d) -> p (r s) d", d=HD)
            g_of = lambda t: t[:, None, :].broadcast_to([P, 2 * NR, HD])
            pool.wait_ge(phase_in, 128)
            pool.wait_ge(rows_free, ROWS["dv"] + 4 * NR + 2)
            with pool.Fori(0, DH) as h:
                pool.wait_ge(L["qn_ok"], h + 1)
                pool.tensor_tensor(grp(qn), grp(qn), g_of(q_gain), ALU.mult)
                pool.tensor_tensor(grp(kn), grp(kn), g_of(k_gain), ALU.mult).then_inc(L["qn_gained"], 1)
                pool.wait_ge(L["av_ok"], h * NR + 1)
                pool.tensor_copy(vs[0:TS, :], vd_r[0:TS, NPR, bass.ds(h * EV, EV)]).then_inc(L["vs_ok"], 1)

            for l in range(DEPTH):
                pool.wait_ge(L["nc_out"], l + 1)
                for gs in range(4):
                    dst = O[8 + gs // 2][l, 0, gs % 2].rearrange("(k p) -> k p", p=P)
                    pool.dma_start(dst, nc_rows[:, gs, :]).then_inc(L["nc_stored"], 16)

        @block.tensor
        def _(pe):
            def products(out, lhs_hi, lhs_lo, rhs_hi, rhs_lo, first, last):
                for part in range(len(out)):
                    pe.matmul(out[part], lhs_hi, rhs_hi[part], start=first, stop=False)
                    pe.matmul(out[part], lhs_hi, rhs_lo[part], start=False, stop=False)
                for part in range(len(out)):
                    ins = pe.matmul(out[part], lhs_lo, rhs_hi[part], start=False, stop=last)
                return ins

            h_parts = lambda t, k: [t[:, k, 0:HALF], t[:, k, HALF:T]]

            def rider(name, i, j, half):
                if name in ride:
                    a = ride[name] + 2 * i + j
                    pe.wait_ge(a_lo_ok, 2 * a + half + 1)
                    if half == 0:
                        pe.wait_ge(ada_free, a + 8)
                    out = ps[0:32, 7, 0:BLOCK_COLS]
                    for k in range(KT // 2):
                        c = c_st[:, half * KT // 2 + k, :]
                        pe.matmul(out, c, ablk(a_hi)[:, k, :], start=(half == 0 and k == 0), stop=False)
                        ins = pe.matmul(out, c, ablk(a_lo)[:, k, :], start=False, stop=(half == 1 and k == KT // 2 - 1))
                    ins.then_inc(ada_done, 1)

            def before(name):
                if READ_A[name] > 1:
                    pe.wait_ge(tile_read_a, READ_A[name])
                if READ_D[name] > 2:
                    pe.wait_ge(tile_read_d, READ_D[name])

            def columns(name, parts_hi, parts_lo, kt=KT, widths=(HALF, HALF)):
                before(name)
                with pe.Fori(0, dict(order)[name] // 2) as i:
                    for j in range(2):
                        pe.wait_ge(w_lo_ok, BASE[name] + 2 * i + j + 1)
                        for t in range(2):
                            if name in READ_BY_ACT:
                                pe.wait_ge(tile_read_a, READ_A[name] + 4 * i + 2 * j + t - 1)
                            else:
                                pe.wait_ge(tile_read_d, READ_D[name] + 4 * i + 2 * j + t - 1)
                            s = (TILE[name] + 2 * j + t) % 2
                            out = [ps[:, 2 * s, 0:widths[0]], ps[:, 2 * s + 1, 0:widths[1]]]
                            for k in range(kt):
                                c = slice(t * P, (t + 1) * P)
                                ins = products(out, blk(w_hi, j, kt)[:, k, c], blk(w_lo, j, kt)[:, k, c],
                                               parts_hi(k), parts_lo(k), k == 0, k == kt - 1)
                            ins.then_inc(w_used if t else tile_done, 1)
                            rider(name, i, j, t)

            def rows(name):
                with pe.Fori(0, dict(order)[name] // 2) as i:
                    for j in range(2):
                        pe.wait_ge(w_lo_ok, BASE[name] + 2 * i + j + 1)
                        for r, (c0, m) in enumerate(RT):
                            n = ROWS[name] + 2 * NR * i + NR * j + r
                            pe.wait_ge(rows_free, n + 1)
                            b = 4 + (NR * j + r) % 2
                            out = ps[0:m, b, 0:BLOCK_COLS]
                            for k in range(KT):
                                hh, hl = h_hi[:, k, c0:c0 + m], h_lo[:, k, c0:c0 + m]
                                wh, wl = blk(w_hi, j)[:, k, :], blk(w_lo, j)[:, k, :]
                                pe.matmul(out, hh, wh, start=(k == 0), stop=False)
                                pe.matmul(out, hh, wl, start=False, stop=False)
                                ins = pe.matmul(out, hl, wh, start=False, stop=(k == KT - 1))
                            ins.then_inc(w_used if r == NR - 1 else rows_done, 1)
                            if r in (1, NR - 1):
                                rider(name, i, j, int(r > 1))

            def norm(which):
                t = TILE["norm%d" % which]
                before("norm%d" % which)
                for k in range(KT):
                    pe.wait_ge(sq_ok, which * KT + k + 1)
                    pe.matmul(slot(t, 0), ones[:, :], sq[:, k % 2, 0:HALF], start=(k == 0), stop=(k == KT - 1))
                    pe.matmul(slot(t, 1), ones[:, :], sq[:, k % 2, HALF:T], start=(k == 0), stop=(k == KT - 1)) \
                      .then_inc(sq_used if k < KT - 1 else tile_done, 1)

            pe.wait_ge(consts, 7)
            pe.wait_ge(vec_in, 16 * (5 + 3 * DEPTH))
            sizes = [2 * KT, 4 * KT, DEPTH * ADA_TILES] + [2 * FT] * (6 * DEPTH)
            for v, m in enumerate(sizes):
                ins = pe.transpose(ps[:, v // 4, (v % 4) * P:(v % 4) * P + m], vec_rows[0:m, v, :], ident[0:m, 0:m])
            ins.then_inc(turned, 1)
            pe.wait_ge(const_in, 32)
            for k in range(KT):
                if k >= 2:
                    pe.wait_ge(x_loaded, k - 1)
                for r in range(NPR):
                    ins = pe.transpose(ps[:, 4 + k % 2, r * P:(r + 1) * P], x_rows[:, r, k * P:(k + 1) * P], ident[:, :])
                ins = pe.transpose(ps[:, 6, k * TS:(k + 1) * TS], x_rows[0:TS, NPR, k * P:(k + 1) * P], ident[0:TS, 0:TS])
                ins.then_inc(turned, 1)

            pe.sem_inc(ada_done, 1)
            pe.wait_ge(c_st_ok, 1)

            def ada_main(i):
                for j in range(2):
                    n = 2 * i + j
                    pe.wait_ge(w_lo_ok, n + 1)
                    if not (isinstance(n, int) and n < 1):
                        pe.wait_ge(ada_free, n)
                    out = ps[0:32, 7, 0:BLOCK_COLS]
                    for k in range(KT):
                        pe.matmul(out, c_st[:, k, :], blk(w_hi, j)[:, k, :], start=(k == 0), stop=False)
                        ins = pe.matmul(out, c_st[:, k, :], blk(w_lo, j)[:, k, :], start=False, stop=(k == KT - 1))
                    ins.then_inc(w_used, 1)

            ada_main(0)
            with pe.Fori(1, 4) as i:
                ada_main(i)

            def h_wait(which):
                pe.wait_ge(h_ok, (which + 1) * KT)

            pe.wait_ge(turned_out, 1)
            norm(0)
            h_wait(0)
            columns("qk", lambda k: h_parts(h_hi, k), lambda k: h_parts(h_lo, k))
            t = TILE["alow"]
            pe.wait_ge(L["aw_ok"], 1)
            before("alow")
            for k in range(KT):
                ins = products([slot(t, 0, m=RANK), slot(t, 1, m=RANK)], aw_hi[:, k, :], aw_lo[:, k, :],
                               h_parts(h_hi, k), h_parts(h_lo, k), k == 0, k == KT - 1)
            ins.then_inc(tile_done, 1)
            pe.wait_ge(x_loaded, KT - 1)
            rows("v")
            rows("r")

            before("gout")
            pe.wait_ge(rows_free, ROWS["dq"] + 2)
            for r, (c0, m) in enumerate(RT):
                nch = max(1, m // CHUNK)
                C = m // nch
                if r:
                    pe.wait_ge(L["on_ok"], r)
                pe.matmul(ps[0:m, 4, :], alT[:, c0:c0 + m], w_alpha[:, :], start=True, stop=True).then_inc(L["logit_ok"], 1)
                pe.wait_ge(L["g_ok"], r + 1)
                if r:
                    pe.wait_ge(L["s2_ok"], r)
                for h in range(GH):
                    ins = pe.matmul(ps[:, 5, h * m:(h + 1) * m], tA[0:m, h * P:(h + 1) * P], cum[0:m, 0:m], start=True, stop=True)
                ins.then_inc(L["b_ok"], 1)
                pe.wait_ge(L["qe_ok"], r + 1)
                for h in range(GH):
                    ins = pe.transpose(ps[0:m, 6, h * P:(h + 1) * P], tC[:, h * m:(h + 1) * m], ident[:, :])
                ins.then_inc(L["kd_turned"], 1)
                if r:
                    pe.wait_ge(L["on_lo"], r)
                if r == 0:
                    pe.wait_ge(L["s_zero"], 1)
                for h in range(GH):
                    ins = pe.matmul(ps[0:m, 0, h * m:(h + 1) * m], tB[:, h * m:(h + 1) * m], qe[:, h * m:(h + 1) * m],
                                    start=True, stop=True)
                ins.then_inc(L["attn_ok"], 1)
                pe.wait_ge(L["kd_out"], r + 1)
                pe.wait_ge(L["b_sb_ok"], r + 1)
                for c in range(nch):
                    for h in range(GH):
                        b = [[1, 2], [3, 5]][c][h // 2]
                        ins = pe.matmul(ps[:, b, (h % 2) * DV:(h % 2 + 1) * DV], kd_r[c * C:(c + 1) * C, h * P:(h + 1) * P],
                                        v_r[c * C:(c + 1) * C, r, h * DV:(h + 1) * DV], start=True, stop=True)
                ins.then_inc(L["u_ok"], 1)
                pe.wait_ge(L["attn_out"], r + 1)
                pe.wait_ge(L["s1_ok"], r + 1)
                s0 = 2 * r if r < NPR else 2 * NPR + 1
                for h in range(GH):
                    b = [4, 6][h // 2]
                    o = slice((h % 2) * DV, (h % 2 + 1) * DV)
                    pe.matmul(ps[0:m, b, o], att[0:m, h * m:(h + 1) * m], v_r[0:m, r, h * DV:(h + 1) * DV],
                              start=True, stop=False, skip_group_check=True)
                    for c in range(nch):
                        ins = pe.matmul(ps[c * C:(c + 1) * C, b, o], qe[:, h * m + c * C:h * m + (c + 1) * C],
                                        S[:, (s0 + c) % 3, h, :], start=False, stop=(c == nch - 1), skip_group_check=True)
                ins.then_inc(L["o_ok"], 1)
                pe.wait_ge(L["on_ok"], r + 1)
                for k in range(KT):
                    ins = pe.transpose(ps[:, k // 4, (k % 4) * m:(k % 4 + 1) * m], r_r[0:m, r, k * P:(k + 1) * P], ident[0:m, 0:m])
                ins.then_inc(L["on_turned"], 1)
            pe.wait_ge(L["on_lo"], NR)
            columns("gout", lambda k: h_parts(h_hi, k), lambda k: h_parts(h_lo, k))

            def ffn(l):
                norm(2 * l + 1)
                h_wait(2 * l + 1)
                for kind, c in ffn_order:
                    if kind == "up":
                        columns((l, kind, c), lambda k: h_parts(h_hi, k), lambda k: h_parts(h_lo, k))
                    else:
                        pe.wait_ge(act_ok, l * FT + sum(CH[:c + 1]))
                        cp = lambda t: (lambda k: [t[:, c % 2, k, 0:HALF], t[:, c % 2, k, HALF:W]])
                        columns((l, kind, c), cp(act_hi), cp(act_lo), kt=CH[c], widths=(HALF, W - HALF))
                if l:
                    pe.wait_ge(L["nc_out"], l)
                for gs in range(4):
                    ins = pe.transpose(ps[0:2 * FT, 6, gs * P:(gs + 1) * P], new_conv[:, :, gs], ident[:, :])
                ins.then_inc(L["nc_turned"], 1)

            ffn(0)

            norm(2)
            h_wait(2)
            for name in ("dq", "dk", "dv"):
                rows(name)
            pe.wait_ge(rows_free, ROWS["dv"] + 4 * NR + 2)
            pe.sem_inc(L["heads_turned"], 1)
            pe.sem_inc(L["av_ok"], 1)
            pe.sem_inc(L["a_turned"], 1)
            with pe.Fori(0, DH) as h:
                pe.wait_ge(L["qn_gained"], h + 1)
                pe.wait_ge(L["kc_in"], 16 * h + 16)
                pe.wait_ge(L["av_out"], NR * h + 1)
                for r, (c0, m) in enumerate(RT[:NPR]):
                    pe.transpose(ps[:, 0, c0:c0 + m], qn[:, r, :], ident[:, :])
                    pe.transpose(ps[:, 1, c0:c0 + m], kn[:, r, :], ident[:, :])
                pe.transpose(ps[:, 3, 0:TS], qn[0:TS, NPR, :], ident[0:TS, 0:TS])
                pe.transpose(ps[:, 3, TS:2 * TS], kn[0:TS, NPR, :], ident[0:TS, 0:TS])
                for r in range(NPAST):
                    ins = pe.transpose(ps[:, 2, r * P:(r + 1) * P], kc[:, r, :], ident[:, :])
                ins.then_inc(L["heads_turned"], 1)
                pe.wait_ge(L["heads_outA"], h + 1)
                pe.wait_ge(L["heads_outD"], h + 1)

                def scores(r):
                    c0, m = RT[r]
                    b = 4 + 2 * (r % 2)
                    if r == NPR:
                        pe.wait_ge(consts, 7)
                    if r >= 2:
                        pe.wait_ge(L["p_ok"], h * NR + r - 1)
                    for c in range(2):
                        s = slice(c * HD, (c + 1) * HD)
                        q = qT[s, c0:c0 + m]
                        if r < NPR:
                            nk = (r + 1) * P
                            pe.matmul(ps[:, b + c, nk - P:nk], low_rows[:, :], neg_cols[:, :], start=True, stop=False,
                                      skip_group_check=True)
                            ins = pe.matmul(ps[:, b + c, 0:nk], q, kT[s, 0:nk], start=False, stop=True, skip_group_check=True)
                        else:
                            pe.matmul(ps[0:m, b + c, 0:PAST], q, kcT[s, :], start=True, stop=True)
                            ins = pe.matmul(ps[0:m, 3 - c, 0:TS], q, kT[s, TP:T], start=True, stop=True)
                    ins.then_inc(L["sc_ok"], 1)

                scores(0)
                for r, (c0, m) in enumerate(RT):
                    n = h * NR + r
                    if r + 1 < NR:
                        scores(r + 1)
                    nb = r + 1 if r < NPR else NPAST + 1
                    if r < NPR:
                        pe.wait_ge(L["a_ok"], n + 1)
                    for b in range(nb):
                        kw = TS if r == NPR and b == NPAST else P
                        ins = pe.transpose(ps[0:kw, 0, b * m:(b + 1) * m], pr[0:m, r % 2, 0, b * P:b * P + kw], ident[0:m, 0:m])
                    ins.then_inc(L["a_turned"], 1)
                    pe.wait_ge(L["a_out"], n + 1)
                    if r == NPR - 1:
                        pe.wait_ge(L["a_ok"], n + 2)
                    if r:
                        pe.wait_ge(L["av_out"], n + 1)
                    if r == NPR:
                        pe.wait_ge(L["kc_in2"], 16 * h + 16)
                        pe.wait_ge(L["vs_ok"], h + 1)
                    for b in range(nb):
                        if r < NPR:
                            lhs, rhs = aT[:, b * m:(b + 1) * m], vd_r[:, b, bass.ds(h * EV, EV)]
                        elif b < NPAST:
                            lhs, rhs = aT[:, b * m:(b + 1) * m], vc[:, b, :]
                        else:
                            lhs, rhs = aT[0:TS, b * m:(b + 1) * m], vs[0:TS, :]
                        ins = pe.matmul(ps[0:m, 1, 0:EV], lhs, rhs, start=(b == 0), stop=(b == nb - 1))
                    ins.then_inc(L["av_ok"], 1)
            for r, (c0, m) in enumerate(RT):
                pe.wait_ge(L["on3_ok"], r + 1)
                if r:
                    pe.wait_ge(L["on_lo"], NR + r)
                else:
                    pe.wait_ge(L["av_out"], NR * DH + 1)
                for k in range(KT):
                    ins = pe.transpose(ps[:, k // 4, (k % 4) * m:(k % 4 + 1) * m], q_r[0:m, r, k * P:(k + 1) * P], ident[0:m, 0:m])
                ins.then_inc(L["on_turned"], 1)
            pe.wait_ge(L["on_lo"], 2 * NR)
            columns("dout", lambda k: h_parts(h_hi, k), lambda k: h_parts(h_lo, k))
            ffn(1)

            pe.wait_ge(tile_read_d, READ_D["end"])
            for r, (c0, m) in enumerate(RT):
                if r >= 2:
                    pe.wait_ge(L["fin_out"], r - 1)
                for k in range(KT):
                    b = 2 * (r % 2) + k // 4
                    ins = pe.transpose(ps[0:m, b, (k % 4) * P:(k % 4 + 1) * P], xT[:, k, c0:c0 + m], ident[:, :])
                ins.then_inc(L["fin_turned"], 1)


        @block.scalar
        def _(act):
            step = Steps(act, act_step)
            A_ = act.activation

            def split(i, j, n0):
                if not (isinstance(i, int) and n0 + 2 * i + j < 2):
                    act.wait_ge(w_used, n0 + 2 * i + j - 1)
                act.wait_ge(w_in[j], 16 * i + 8 * n0 + 16)
                act.copy(w_hi[:, j, :], w_raw[:, j, :]).then_inc(w_hi_ok, 1)

            def next_split(name, i, j):
                split(i + 1 if j else i, 1 - j, BASE[name])

            def rider(name, i, j, half):
                if name in ride:
                    a = 2 * (ride[name] + 2 * i + j) + half
                    act.wait_ge(ada_done, a + 1)
                    act.wait_ge(a_in, 64 * i + 16 * (2 * (ride[name] + j) + half + 1))
                    act.copy(a_hi[:, :], a_raw[:, :]).then_inc(a_hi_ok, 1)

            def over(name, body, last=False):
                pairs = dict(order)[name] // 2
                with act.Fori(0, pairs - last) as i:
                    for j in range(2):
                        rider(name, i, j, 0)
                        next_split(name, i, j)
                        body(i, j, lambda: rider(name, i, j, 1))
                if last:
                    next_split(name, pairs - 1, 0)
                    body(pairs - 1, 0, lambda: None)
                    body(pairs - 1, 1, lambda: None)

            def summed(name, i, j, t):
                if t:
                    act.wait_ge(w_used, BASE[name] + 2 * i + j + 1)
                else:
                    act.wait_ge(tile_done, FIRST[name] + 2 * i + j + 1)

            def row_summed(name, i, j, r):
                if r == NR - 1:
                    act.wait_ge(w_used, BASE[name] + 2 * i + j + 1)
                else:
                    act.wait_ge(rows_done, FIRST_ROWS[name] + (NR - 1) * (2 * i + j) + r + 1)

            act.wait_ge(turned, 1)
            entry = lambda v, m: ps[:, v // 4, (v % 4) * P:(v % 4) * P + m]
            step.then(A_(cs[:, :], entry(0, 2 * KT), ACT.Silu))
            act.copy(norm_g[:, :, :], entry(1, 4 * KT).rearrange("p (l k) -> p l k", k=KT)).then_inc(tile_read_a, 1)
            act.copy(b_ada[:, :, :], entry(2, DEPTH * ADA_TILES).rearrange("p (l k) -> p l k", k=ADA_TILES))
            v = 3
            while v < 3 + 6 * DEPTH:
                e = min(3 + 6 * DEPTH, (v // 4 + 1) * 4)
                src = ps[:, v // 4, (v % 4) * P:(v % 4 + e - v) * P].rearrange("p (v m) -> p v m", m=P)[:, :, 0:2 * FT]
                ins = act.copy(conv_c[:, v - 3:e - 3, :], src)
                v = e
            ins.then_inc(turned_out, 1)
            act.wait_ge(consts, 7)
            act.wait_ge(c_hi_ok, 1)
            act.copy(c_st[:, :, 0:2], cs[:, :].rearrange("p (g k) -> p k g", g=2)).then_inc(c_hi_ok, 1)
            for k in range(KT):
                act.wait_ge(turned, k + 2)
                act.copy(xT[:, k, 0:TP], ps[:, 4 + k % 2, :]).then_inc(x_loaded if k < KT - 2 else rows_free, 1)
            act.copy(xT[:, :, TP:T], ps[:, 6, 0:KT * TS].rearrange("p (k t) -> p k t", t=TS)).then_inc(x_loaded, 1)

            split(0, 0, 0)
            next_split("ada0", 0, 0)
            next_split("ada0", 0, 1)
            with act.Fori(1, 4) as i:
                next_split("ada0", i, 0)
                next_split("ada0", i, 1)

            def norm(which):
                if which:
                    act.wait_ge(tile_read_d, READ_D["norm%d" % which])
                else:
                    act.wait_ge(x_loaded, KT - 1)
                for k in range(KT):
                    if k >= 2:
                        act.wait_ge(sq_used, which * (KT - 1) + k - 1)
                    elif which:
                        act.wait_ge(h_ok, which * KT)
                    A_(sq[:, k % 2, :], xT[:, k, :], ACT.Square).then_inc(sq_ok, 1)
                act.wait_ge(tile_done, FIRST["norm%d" % which] + 1)
                t = TILE["norm%d" % which]
                if which:
                    act.wait_ge(rms_used, which)
                A_(rstd[:, 0:HALF], slot(t, 0), ACT.Sqrt, bias=eps[:, :], scale=1.0 / D)
                A_(rstd[:, HALF:T], slot(t, 1), ACT.Sqrt, bias=eps[:, :], scale=1.0 / D).then_inc(tile_read_a, 1)
                user = ["qk", (0, "up", 0), "dq", (1, "up", 0)][which]
                act.wait_ge(w_used, BASE[user])
                for k in range(KT):
                    act.wait_ge(xs_ok, which * KT + k + 1)
                    A_(h_hi[:, k, 0:TP], sq[:, k % 2, 0:TP], ACT.Identity, bias=shift[:, k, 0:1])
                    A_(h_hi[:, k, TP:T], sq[:, k % 2, TP:T], ACT.Identity, bias=shift[:, k, 1:2]).then_inc(h_hi_ok, 1)

            norm(0)

            def qk_out(i, j, ride2):
                for t in range(2):
                    if t:
                        ride2()
                    summed("qk", i, j, t)
                    s = (TILE["qk"] + 2 * j + t) % 2
                    m = 4 * i + 2 * j + t
                    act.copy(qk[:, bass.ds(m, 1), 0:HALF], ps[:, 2 * s, None, 0:HALF])
                    act.copy(qk[:, bass.ds(m, 1), HALF:T], ps[:, 2 * s + 1, None, 0:HALF]).then_inc(tile_read_a, 1)

            over("qk", qk_out)
            act.wait_ge(phase_in, 64)
            act.copy(aw_hi[:, :, :], aw[:, :, :]).then_inc(L["aw_hi_ok"], 1)
            act.wait_ge(tile_done, FIRST["alow"] + 1)
            t = TILE["alow"]
            act.wait_ge(L["al_ok"], 1)
            act.copy(alT[0:RANK, 0:HALF], slot(t, 0, m=RANK))
            act.copy(alT[0:RANK, HALF:T], slot(t, 1, m=RANK)).then_inc(tile_read_a, 1)

            def rows_out(name, dst, func):
                def body(i, j, ride2):
                    for r, (c0, m) in enumerate(RT):
                        if r == 2:
                            ride2()
                        row_summed(name, i, j, r)
                        A_(dst[0:m, r, bass.ds((2 * i + j) * BLOCK_COLS, BLOCK_COLS)], ps[0:m, 4 + (NR * j + r) % 2, 0:BLOCK_COLS],
                           func).then_inc(rows_free, 1)
                over(name, body)

            rows_out("v", v_r, ACT.Copy)
            rows_out("r", r_r, ACT.Silu)

            for r, (c0, m) in enumerate(RT):
                nch = max(1, m // CHUNK)
                n = GH * m
                act.wait_ge(L["logit_ok"], r + 1)
                if r:
                    act.wait_ge(L["attn_ok"], r)
                A_(tB[0:m, :], ps[0:m, 4, :], ACT.Abs).then_inc(L["logit_out"], 1)
                act.wait_ge(L["logit_out"], r + 1)
                step.then(A_(tB[0:m, :], tB[0:m, :], ACT.Exp, scale=-1.0))
                A_(tB[0:m, :], tB[0:m, :], ACT.Ln, bias=1.0).then_inc(L["lsp_ok"], 1)
                act.wait_ge(L["bd_ok"], r + 1)
                if r:
                    act.wait_ge(L["o_ok"], r)
                last = tA[:, 0:n].rearrange("p (h c t) -> p h c t", h=GH, c=nch)[:, :, :, m // nch - 1]
                A_(dec[:, :, 0:nch], last, ACT.Exp)
                A_(qe[:, 0:n], tA[:, 0:n], ACT.Exp)
                A_(tB[:, 0:n], tA[:, 0:n], ACT.Exp, scale=-1.0)
                A_(tC[:, 0:n], tC[:, 0:n], ACT.Exp, scale=-1.0).then_inc(L["exp_ok"], 1)
                act.wait_ge(L["kd_turned"], r + 1)
                if r:
                    act.wait_ge(L["u_ok"], r)
                act.copy(kd_r[0:m, :], ps[0:m, 6, :]).then_inc(L["kd_out"], 1)
                act.wait_ge(L["o_ok"], r + 1)
                for h in range(GH):
                    ins = A_([tA, kd_r][h // 2][0:m, (h % 2) * DV:(h % 2 + 1) * DV], ps[0:m, [4, 6][h // 2], (h % 2) * DV:(h % 2 + 1) * DV], ACT.Square,
                             accum_out=stat[0:m, h:h + 1])
                step.then(ins)
                A_(stat[0:m, 4:4 + GH], stat[0:m, 0:GH], ACT.Sqrt, bias=eps[0:m, :], scale=1.0 / DV).then_inc(L["oss_ok"], 1)
                act.wait_ge(L["on_turned"], r + 1)
                if r == 0:
                    act.wait_ge(w_used, BASE["gout"])
                for b in range(2):
                    ins = act.copy(h_hi[:, 4 * b:4 * b + 4, c0:c0 + m], ps[:, b, 0:4 * m].rearrange("p (k t) -> p k t", k=4))
                ins.then_inc(L["on_hi"], 1)
            over("gout", lambda i, j, ride2: ride2())

            def ffn(l):
                norm(2 * l + 1)
                if l:
                    act.wait_ge(L["nc_turned"], l)
                else:
                    act.wait_ge(state_out, 32)
                done = {"up": 0}
                for kind, c in ffn_order:
                    name = (l, kind, c)
                    last = l == DEPTH - 1 and (kind, c) == ffn_order[-1]
                    if kind == "down":
                        over(name, lambda i, j, ride2: ride2(), last=last)
                        continue
                    c0 = sum(CH[:c])
                    u0 = 2 * c0
                    if c >= 2:
                        act.wait_ge(w_used, BASE[(l, "down", c - 2)] + nblk("down", c - 2))

                    def body(i, j, ride2):
                        for t in range(2):
                            if t:
                                ride2()
                            u = u0 + 4 * i + 2 * j + t
                            summed(name, i, j, t)
                            act.wait_ge(conv_ok, l * (2 * FT * 1 + 2) + u + 1)
                            s = (TILE[name] + 2 * j + t) % 2
                            ft = j * FT + c0 + 2 * i + t
                            act.copy(up[:, t, 2:2 + HALF], ps[:, 2 * s, 0:HALF])
                            act.copy(up[:, t, 2 + HALF:2 + TP], ps[:, 2 * s + 1, 0:PB])
                            act.copy(up[:, t, TP + 4:T + 4], ps[:, 2 * s + 1, PB:HALF])
                            act.copy(up[:, t, TP + 2:TP + 4], conv_c[:, 6 * l + 4:6 * l + 6, bass.ds(ft, 1)].rearrange("p a b -> p (a b)"))
                            ends = ps[:, 2 * s + 1, PB - 2:PB - 2 + 2 * TS].rearrange("p (g t) -> p g t", g=2)[:, :, 0:2]
                            act.copy(new_conv[:, bass.ds(ft, 1), :].rearrange("p a (g t) -> p (a g) t", g=2), ends).then_inc(tile_read_a, 1)
                            act.wait_ge(tile_read_a, READ_A[name] + 4 * i + 2 * j + t + 1)
                            A_(cv1[:, t, :], up[:, t, 0:W], ACT.Identity, scale=conv_c[:, 6 * l, bass.ds(ft, 1)],
                               bias=conv_c[:, 6 * l + 3, bass.ds(ft, 1)]).then_inc(up_ok, 1)
                            if j:
                                pr_n = l * FT + c0 + 2 * i + t
                                act.wait_ge(conv_ok, l * (2 * FT + 2) + u + 3)
                                A_(cv[:, 1, t, :], cv[:, 1, t, :], ACT.Silu).then_inc(silu_ok, 1)
                                act.wait_ge(prod_ok, pr_n + 1)
                                act.copy(act_hi[:, c % 2, bass.ds(2 * i + t, 1), :], cv[:, 0, t, None, :]).then_inc(act_hi_ok, 1)
                    over(name, body)

            ffn(0)

            norm(2)

            def qkv_out(name, dst, which):
                def body(i, j, ride2):
                    for r, (c0, m) in enumerate(RT):
                        if r == 2:
                            ride2()
                        row_summed(name, i, j, r)
                        src = ps[0:m, 4 + (NR * j + r) % 2, 0:BLOCK_COLS]
                        if which < 2:
                            k = which * 4 * NR + 2 * NR * i + NR * j + r
                            act.wait_ge(L["ssq_used"], k + 1)
                            b = (NR * j + r) % 2
                            A_(ssq[0:m, b * BLOCK_COLS:(b + 1) * BLOCK_COLS], src, ACT.Square).then_inc(L["ssq_ok"], 1)
                        A_(dst[0:m, r, bass.ds((2 * i + j) * BLOCK_COLS, BLOCK_COLS)], src, ACT.Copy).then_inc(rows_free, 1)
                over(name, body)

            qkv_out("dq", q_r, 0)
            qkv_out("dk", k_r, 1)
            act.wait_ge(L["ssq_used"], 2 + 8 * NR)
            A_(rs[:, :, :, :], ss[:, :, :, :], ACT.Sqrt, bias=eps[:, :], scale=1.0 / HD).then_inc(L["rs_ok"], 1)
            qkv_out("dv", vd_r, 2)
            act.wait_ge(L["lam_ok"], 1)
            A_(stat[:, 34:36], stat[:, 32:34], ACT.Exp).then_inc(L["lam_ok"], 1)
            act.sem_inc(L["av_out"], 1)
            with act.Fori(0, DH) as h:
                act.wait_ge(L["heads_turned"], h + 2)
                act.copy(qT[:, 0:TP], ps[:, 0, :])
                act.copy(kcT[:, :], ps[:, 2, 0:PAST]).then_inc(L["heads_outA"], 1)

                def exps(r):
                    c0, m = RT[r]
                    n = h * NR + r
                    if r == 0:
                        act.wait_ge(L["a_turned"], n + 1)
                    elif r >= 2:
                        act.wait_ge(L["a_turned"], n)
                    act.wait_ge(L["mx_ok"], n + 1)
                    s0 = 8 * (r % 2)
                    for c in range(2):
                        b = 4 + 2 * (r % 2) + c
                        nk = (r + 1) * P if r < NPR else PAST
                        ins = A_(pr[0:m, r % 2, c, 0:nk], ps[0:m, b, 0:nk], ACT.Exp, scale=SCALE, bias=stat[0:m, s0 + c:s0 + c + 1],
                                 accum_out=stat[0:m, s0 + 2 + c:s0 + 3 + c])
                        if r == NPR:
                            ins = A_(pr[0:m, r % 2, c, PAST:PAST + TS], ps[0:m, 3 - c, 0:TS], ACT.Exp, scale=SCALE,
                                     bias=stat[0:m, s0 + c:s0 + c + 1], accum_out=stat[0:m, s0 + 4 + c:s0 + 5 + c])
                    ins.then_inc(L["p_ok"], 1)

                exps(0)
                for r, (c0, m) in enumerate(RT):
                    n = h * NR + r
                    if r + 1 < NR:
                        exps(r + 1)
                    nb = r + 1 if r < NPR else NPAST
                    act.wait_ge(L["a_turned"], n + 2)
                    act.wait_ge(L["av_ok"], n + 1)
                    ins = act.copy(aT[:, 0:nb * m], ps[:, 0, 0:nb * m])
                    if r == NPR:
                        ins = act.copy(aT[0:TS, nb * m:(nb + 1) * m], ps[0:TS, 0, nb * m:(nb + 1) * m])
                    ins.then_inc(L["a_out"], 1)
                    act.wait_ge(L["av_ok"], n + 2)
                    act.copy(q_r[0:m, r, bass.ds(h * EV, EV)], ps[0:m, 1, 0:EV])
                    A_(osq[0:m, :], ps[0:m, 1, 0:EV], ACT.Square, accum_out=oss[0:m, r, bass.ds(h, 1)]).then_inc(L["av_out"], 1)
                    act.wait_ge(L["av_out"], n + 2)
            A_(ors[:, :, :], oss[:, :, :], ACT.Sqrt, bias=eps[:, :], scale=1.0 / EV).then_inc(L["osq_ok"], 1)
            for r, (c0, m) in enumerate(RT):
                act.wait_ge(L["on_turned"], NR + r + 1)
                for b in range(2):
                    ins = act.copy(h_hi[:, 4 * b:4 * b + 4, c0:c0 + m], ps[:, b, 0:4 * m].rearrange("p (k t) -> p k t", k=4))
                ins.then_inc(L["on_hi"], 1)
            over("dout", lambda i, j, ride2: ride2())
            ffn(1)
            for r, (c0, m) in enumerate(RT):
                act.wait_ge(L["fin_turned"], r + 1)
                if r >= 2:
                    act.wait_ge(L["fin_stored%d" % (r % 2)], 16 * (r // 2))
                for b in range(2):
                    ins = act.copy(y_rows[0:m, r % 2, b * 512:(b + 1) * 512], ps[0:m, 2 * (r % 2) + b, :])
                ins.then_inc(L["fin_out"], 1)

        @block.vector
        def _(dve):
            step = Steps(dve, dve_step)
            TT, STT = dve.tensor_tensor, dve.scalar_tensor_tensor
            f32 = lambda ap: ap.bitcast(F32)

            def split(i, j, n0):
                dve.wait_ge(w_hi_ok, n0 + 2 * i + j + 1)
                TT(w_lo[:, j, :], w_raw[:, j, :], f32(w_hi[:, j, :]), ALU.subtract).then_inc(w_lo_ok, 1)

            def next_split(name, i, j):
                split(i + 1 if j else i, 1 - j, BASE[name])

            def ada_out(l, b):
                dve.transpose(ada_t[:, :], ps[0:32, 7, 0:BLOCK_COLS]).then_inc(ada_free, 1)

            def ada_sum(l, b, done):
                dve.wait_ge(ada_free, done)
                v = ada_t[:, :].rearrange("p (t q c) -> p t q c", t=2, q=4)
                for q in range(4):
                    ins = TT(ada[32 * q:32 * q + 32, l, bass.ds(2 * b, 2), :], v[:, :, q, 0:2], v[:, :, q, 2:4], ALU.add)
                step.then(ins)

            def over(name, body, last=False, per=0):
                pairs = dict(order)[name] // 2
                riding = name in ride
                with dve.Fori(0, pairs - last) as i:
                    step.loop(i, per + 2 * riding)
                    for j in range(2):
                        def rider(half):
                            if riding:
                                dve.wait_ge(a_hi_ok, 2 * (ride[name] + 2 * i + j) + half + 1)
                                TT(a_lo[:, :], a_raw[:, :], f32(a_hi[:, :]), ALU.subtract).then_inc(a_lo_ok, 1)

                        rider(0)
                        next_split(name, i, j)
                        body(i, j, lambda: rider(1))
                        if riding:
                            a = ride[name] + 2 * i + j
                            l, b0 = shared_ride(name)
                            dve.wait_ge(ada_done, 2 * a + 3)
                            ada_out(l, b0 + 2 * i + j)
                            ada_sum(l, b0 + 2 * i + j, a + 9)
                step.end(pairs - last)
                if last:
                    next_split(name, pairs - 1, 0)
                    body(pairs - 1, 0, lambda: None)
                    body(pairs - 1, 1, lambda: None)

            dve.memset(c_st[:, :, :].bitcast(F32), 0.0).then_inc(c_hi_ok, 1)
            dve.wait_ge(c_hi_ok, 2)
            TT(c_st[:, :, 2:4], cs[:, :].rearrange("p (g k) -> p k g", g=2), f32(c_st[:, :, 0:2]), ALU.subtract).then_inc(c_st_ok, 1)
            split(0, 0, 0)

            def ada_main(i):
                for j in range(2):
                    next_split("ada0", i, j)
                    dve.wait_ge(w_used, 2 * i + j + 1)
                    ada_out(0, 2 * i + j)
                    ada_sum(0, 2 * i + j, 2 * i + j + 1)

            ada_main(0)
            with dve.Fori(1, 4) as i:
                step.at, step.n, before_loop = (i - 1) * 2 + step.n, 0, step.n
                ada_main(i)
            step.at, step.n = before_loop + 6, 0

            def add_bias(dst, l, first):
                b = b_ada[:, l, first * KT:(first + 1) * KT, None].broadcast_to([P, KT, 2])
                step.then(TT(dst[:, :, :], ada[:, l, first * KT:(first + 1) * KT, :], b, ALU.add))

            def norm(which):
                l, sub = which // 2, which % 2
                add_bias(shift, l, 3 * sub)
                add_bias(gain, l, 3 * sub + 1)
                ng = norm_g[:, 2 * sub + l, :, None].broadcast_to([P, KT, 2])
                step.then(STT(out=gain[:, :, :], in0=gain[:, :, :], scalar=1.0, in1=ng, op0=ALU.add, op1=ALU.mult))
                dve.wait_ge(tile_read_a, READ_A["norm%d" % which] + 1)
                dve.reciprocal(rstd[:, :], rstd[:, :]).then_inc(rms_used, 1)
                dve.wait_ge(rms_used, which + 1)
                for k in range(KT):
                    if k >= 2:
                        dve.wait_ge(h_ok, which * KT + k - 1)
                    for gq, c in ((0, slice(0, TP)), (1, slice(TP, T))):
                        ins = STT(out=sq[:, k % 2, c], in0=xT[:, k, c], scalar=gain[:, k, gq:gq + 1], in1=rstd[:, c],
                                  op0=ALU.mult, op1=ALU.mult)
                    ins.then_inc(xs_ok, 1)
                    dve.wait_ge(h_hi_ok, which * KT + k + 1)
                    for gq, c in ((0, slice(0, TP)), (1, slice(TP, T))):
                        ins = STT(out=h_lo[:, k, c], in0=sq[:, k % 2, c], scalar=shift[:, k, gq:gq + 1], in1=f32(h_hi[:, k, c]),
                                  op0=ALU.add, op1=ALU.subtract)
                    ins.then_inc(h_ok, 1)

            def stream_out(name, junk):
                def body(i, j, ride2):
                    for t in range(2):
                        if t:
                            ride2()
                            dve.wait_ge(w_used, BASE[name] + 2 * i + j + 1)
                        else:
                            dve.wait_ge(tile_done, FIRST[name] + 2 * i + j + 1)
                        dve.wait_ge(tile_read_d, READ_D[name] + 4 * i + 2 * j + t)
                        s = (TILE[name] + 2 * j + t) % 2
                        m = 4 * i + 2 * j + t
                        for gq, c, b, c1 in ((0, slice(0, HALF), 0, 0), (0, slice(HALF, TP), 1, 0), (1, slice(TP, T), 1, PB + junk)):
                            x = xT[:, bass.ds(m, 1), c].rearrange("p a t -> p (a t)")
                            ins = STT(out=x, in0=ps[:, 2 * s + b, c1:c1 + c.stop - c.start],
                                      scalar=gate[:, bass.ds(m, 1), gq:gq + 1].rearrange("p a t -> p (a t)"), in1=x,
                                      op0=ALU.mult, op1=ALU.add)
                        ins.then_inc(tile_read_d, 1)
                return body

            norm(0)
            over("qk", lambda i, j, ride2: ride2())
            dve.wait_ge(L["aw_hi_ok"], 1)
            dve.memset(alT[:, :], 1.0).then_inc(L["al_ok"], 1)
            TT(aw_lo[:, :, :], aw[:, :, :], f32(aw_hi[:, :, :]), ALU.subtract).then_inc(L["aw_ok"], 1)
            over("v", lambda i, j, ride2: ride2())
            over("r", lambda i, j, ride2: ride2())
            dve.wait_ge(w_used, BASE["gout"])
            dve.memset(att[:, :], 0.0)
            dve.memset(S[:, 0, :, :], 0.0).then_inc(L["s_zero"], 1)
            for r, (c0, m) in enumerate(RT):
                nch = max(1, m // CHUNK)
                C = m // nch
                n = GH * m
                hm = lambda t: t[:, 0:n].rearrange("p (h t) -> p h t", h=GH)
                rg = r_r[0:m, r, :].rearrange("p (h e) -> p h e", h=GH)
                if r == 0:
                    dve.wait_ge(rows_free, ROWS["dq"] + 2)
                TT(rg, rg, gla_g[0:m, None, :].broadcast_to([m, GH, DV]), ALU.mult).then_inc(L["dg_ok"], 1)
                dve.wait_ge(L["logit_out"], r + 1)
                step.then(dve.tensor_scalar(tA[0:m, :], ps[0:m, 4, :], 0.0, None, ALU.min))
                dve.wait_ge(L["lsp_ok"], r + 1)
                TT(tA[0:m, :], tA[0:m, :], tB[0:m, :], ALU.subtract).then_inc(L["g_ok"], 1)
                dve.wait_ge(L["b_ok"], r + 1)
                dve.tensor_copy(tA[:, 0:n], ps[:, 5, 0:n]).then_inc(L["b_sb_ok"], 1)
                dve.wait_ge(L["b_sb_ok"], r + 1)
                hc = lambda t: t[:, 0:n].rearrange("p (h t) -> p h t", t=C)
                TT(hc(tC), hc(tA), hc(tA)[:, :, C - 1:C].broadcast_to([P, GH * nch, C]), ALU.subtract).then_inc(L["bd_ok"], 1)
                dve.wait_ge(L["exp_ok"], r + 1)
                q, k = qk[:, 0:GH, c0:c0 + m], qk[:, GH:2 * GH, c0:c0 + m]
                STT(out=hm(qe), in0=q, scalar=DK ** -0.5, in1=hm(qe), op0=ALU.mult, op1=ALU.mult)
                TT(hm(tB), k, hm(tB), ALU.mult)
                TT(hm(tC), k, hm(tC), ALU.mult).then_inc(L["qe_ok"], 1)
                dve.wait_ge(L["attn_ok"], r + 1)
                if r == NPR:
                    dve.wait_ge(L["o_ok"], r)
                    step.then(dve.memset(att[:, :], 0.0))
                if r == 0:
                    dve.wait_ge(L["s_zero"], 1)
                    dve.wait_ge(consts, 7)
                dve.copy_predicated(att[0:m, 0:n].rearrange("p (h t) -> p h t", h=GH),
                                    cum[0:m, None, 0:m].broadcast_to([m, GH, m]).bitcast(U32),
                                    ps[0:m, 0, 0:n].rearrange("p (h t) -> p h t", h=GH)).then_inc(L["attn_out"], 1)
                dve.wait_ge(L["u_ok"], r + 1)
                s0 = 2 * r if r < NPR else 2 * NPR + 1
                if r == NPR:
                    dve.wait_ge(L["s_in"], 16)
                for c in range(nch):
                    for h in range(GH):
                        b = [[1, 2], [3, 5]][c][h // 2]
                        ins = STT(out=S[:, (s0 + c + 1) % 3, h, :], in0=S[:, (s0 + c) % 3, h, :], scalar=dec[:, h, c:c + 1],
                                  in1=ps[:, b, (h % 2) * DV:(h % 2 + 1) * DV], op0=ALU.mult, op1=ALU.add)
                        if nch == 1 and h == GH - 2 or nch > 1 and c == 0 and h == GH - 1:
                            ins.then_inc(L["s1_ok"], 1)
                            if nch > 1:
                                dve.wait_ge(L["s1_ok"], r + 1)
                ins.then_inc(L["s2_ok"], 1)
                dve.wait_ge(L["oss_ok"], r + 1)
                step.then(dve.reciprocal(stat[0:m, 8:8 + GH], stat[0:m, 4:4 + GH]))
                for h in range(GH):
                    ins = STT(out=r_r[0:m, r, h * DV:(h + 1) * DV], in0=ps[0:m, [4, 6][h // 2], (h % 2) * DV:(h % 2 + 1) * DV],
                              scalar=stat[0:m, 8 + h:9 + h], in1=r_r[0:m, r, h * DV:(h + 1) * DV], op0=ALU.mult, op1=ALU.mult)
                ins.then_inc(L["on_ok"], 1)
                dve.wait_ge(L["on_hi"], r + 1)
                for b in range(2):
                    k4 = slice(4 * b, 4 * b + 4)
                    ins = TT(h_lo[:, k4, c0:c0 + m], ps[:, b, 0:4 * m].rearrange("p (k t) -> p k t", k=4), f32(h_hi[:, k4, c0:c0 + m]),
                             ALU.subtract)
                    if r >= NR - 2 and b == 0:
                        ins.then_inc(tile_read_d, 1)
                ins.then_inc(L["on_lo"], 1)
            add_bias(gate, 0, 2)
            over("gout", stream_out("gout", 0))

            def ffn(l):
                norm(2 * l + 1)
                add_bias(gate, l, 5)
                dve.wait_ge(w_used, BASE[(l, "up", 0)])
                if l == 0:
                    dve.wait_ge(state_out, 32)
                for t in range(2):
                    dve.memset(up[:, t, 0:2], 0.0).then_inc(conv_ok, 1)
                for kind, c in ffn_order:
                    name = (l, kind, c)
                    last = l == DEPTH - 1 and (kind, c) == ffn_order[-1]
                    if kind == "down":
                        over(name, stream_out(name, 2), last=last)
                        continue
                    c0 = sum(CH[:c])

                    def body(i, j, ride2):
                        for t in range(2):
                            if t:
                                ride2()
                            ft = j * FT + c0 + 2 * i + t
                            dve.wait_ge(up_ok, l * 2 * FT + 2 * c0 + 4 * i + 2 * j + t + 1)
                            w = lambda n: conv_c[:, 6 * l + n, bass.ds(ft, 1)]
                            step.then(STT(out=cv1[:, t, :], in0=up[:, t, 1:W + 1], scalar=w(1), in1=cv1[:, t, :], op0=ALU.mult, op1=ALU.add))
                            STT(out=cv[:, j, t, :], in0=up[:, t, 2:W + 2], scalar=w(2), in1=cv1[:, t, :], op0=ALU.mult,
                                op1=ALU.add).then_inc(conv_ok, 1)
                            if j:
                                n = l * FT + c0 + 2 * i + t
                                dve.wait_ge(silu_ok, n + 1)
                                TT(cv[:, 0, t, :], cv[:, 1, t, :], cv[:, 0, t, :], ALU.mult).then_inc(prod_ok, 1)
                                dve.wait_ge(act_hi_ok, n + 1)
                                m1 = bass.ds(2 * i + t, 1)
                                TT(act_lo[:, c % 2, m1, :], cv[:, 0, t, None, :], f32(act_hi[:, c % 2, m1, :]), ALU.subtract).then_inc(act_ok, 1)
                    over(name, body, per=4)
                dve.wait_ge(L["nc_turned"], l + 1)
                if l:
                    dve.wait_ge(L["nc_stored"], 64 * l)
                dve.tensor_copy(nc_rows[:, :, :], ps[0:2 * FT, 6, :].rearrange("p (g t) -> p g t", g=4)).then_inc(L["nc_out"], 1)

            ffn(0)

            dve.wait_ge(act_ok, FT)
            dve.memset(q_r[:, NPR, :], 1.0).then_inc(L["ssq_used"], 1)
            dve.memset(k_r[:, NPR, :], 1.0).then_inc(L["ssq_used"], 1)
            dve.memset(oss[:, :, :], 1.0)
            step.then(dve.memset(ss[:, :, :, :], 1.0))
            norm(2)

            def sums(name, which):
                def body(i, j, ride2):
                    for r, (c0, m) in enumerate(RT):
                        k = which * 4 * NR + 2 * NR * i + NR * j + r
                        b = (NR * j + r) % 2
                        if r == 2:
                            ride2()
                        dve.wait_ge(L["ssq_ok"], k + 1)
                        dve.tensor_reduce(ss[0:m, r, which, bass.ds(4 * (2 * i + j), 4)],
                                          ssq[0:m, b * BLOCK_COLS:(b + 1) * BLOCK_COLS].rearrange("p (g d) -> p g d", d=HD),
                                          AX_X, ALU.add).then_inc(L["ssq_used"], 1)
                over(name, body)

            sums("dq", 0)
            sums("dk", 1)
            dve.wait_ge(L["rs_ok"], 1)
            step.then(dve.reciprocal(ss[:, :, :, :], rs[:, :, :, :]))
            over("dv", lambda i, j, ride2: ride2())
            dve.wait_ge(phase_in, 128)
            lp = lam_in[:, :, :].rearrange("p (a b) d -> p a b d", b=2)
            step.then(TT(lp[:, :, 0, :], lp[:, :, 0, :], lp[:, :, 1, :], ALU.mult))
            dve.tensor_reduce(stat[:, 32:34], lp[:, :, 0, :], AX_X, ALU.add).then_inc(L["lam_ok"], 1)
            dve.wait_ge(L["lam_ok"], 2)
            step.then(TT(stat[:, 36:37], stat[:, 35:36], stat[:, 34:35], ALU.subtract))
            step.then(dve.tensor_scalar(stat[:, 37:38], stat[:, 36:37], -LAM_INIT, None, ALU.add))
            step.then(dve.tensor_scalar(d_gain[:, :], d_gain[:, :], 1.0 - LAM_INIT, None, ALU.mult))
            with dve.Fori(0, DH) as h:
                step.loop(h, NR * 4 + 2)
                dve.wait_ge(L["heads_turned"], h + 1)
                dve.wait_ge(L["kn_out"], 32 * h + 1)
                for w, (src, dst) in enumerate(((q_r, qn), (k_r, kn))):
                    s = src[:, :, bass.ds(h * EV, EV)].rearrange("p r (s d) -> p r s d", d=HD)
                    rr = ss[:, :, w, bass.ds(2 * h, 2)][:, :, :, None].broadcast_to([P, NR, 2, HD])
                    ins = TT(dst[:, :, :].rearrange("p r (s d) -> p r s d", d=HD), s, rr, ALU.mult)
                ins.then_inc(L["qn_ok"], 1)
                dve.wait_ge(L["heads_turned"], h + 2)
                dve.tensor_copy(kT[:, 0:TP], ps[:, 1, :])
                dve.tensor_copy(qT[:, TP:T], ps[:, 3, 0:TS])
                dve.tensor_copy(kT[:, TP:T], ps[:, 3, TS:2 * TS]).then_inc(L["heads_outD"], 1)

                def maxima(r):
                    c0, m = RT[r]
                    s0, x0 = 8 * (r % 2), 16 + 4 * (r % 2)
                    dve.wait_ge(L["sc_ok"], h * NR + r + 1)
                    for c in range(2):
                        nk = (r + 1) * P if r < NPR else PAST
                        ins = dve.reduce_max(stat[0:m, x0 + c:x0 + c + 1], ps[0:m, 4 + 2 * (r % 2) + c, 0:nk], AX_X)
                    if r == NPR:
                        for c in range(2):
                            ins = dve.reduce_max(stat[0:m, x0 + 2 + c:x0 + 3 + c], ps[0:m, 3 - c, 0:TS], AX_X)
                        step.then(ins)
                        ins = TT(stat[0:m, x0:x0 + 2], stat[0:m, x0:x0 + 2], stat[0:m, x0 + 2:x0 + 4], ALU.max)
                    step.then(ins)
                    dve.tensor_scalar(stat[0:m, s0:s0 + 2], stat[0:m, x0:x0 + 2], -SCALE, None, ALU.mult).then_inc(L["mx_ok"], 1)

                maxima(0)
                for r, (c0, m) in enumerate(RT):
                    if r + 1 < NR:
                        maxima(r + 1)
                    n = h * NR + r
                    s0 = 8 * (r % 2)
                    nk = (r + 1) * P if r < NPR else PAST + TS
                    dve.wait_ge(L["p_ok"], n + 1)
                    den = stat[0:m, s0 + 2:s0 + 4]
                    if r == NPR:
                        step.then(TT(den, den, stat[0:m, s0 + 4:s0 + 6], ALU.add))
                    step.then(dve.reciprocal(den, den))
                    step.then(TT(den[:, 1:2], den[:, 1:2], stat[0:m, 37:38], ALU.mult))
                    step.then(dve.tensor_scalar(pr[0:m, r % 2, 1, 0:nk], pr[0:m, r % 2, 1, 0:nk], den[:, 1:2], None, ALU.mult))
                    STT(out=pr[0:m, r % 2, 0, 0:nk], in0=pr[0:m, r % 2, 0, 0:nk], scalar=den[:, 0:1], in1=pr[0:m, r % 2, 1, 0:nk],
                        op0=ALU.mult, op1=ALU.add).then_inc(L["a_ok"], 1)
            step.end(DH)
            dve.wait_ge(L["osq_ok"], 1)
            step.then(dve.reciprocal(oss[:, :, :], ors[:, :, :]))
            for r, (c0, m) in enumerate(RT):
                o = q_r[0:m, r, :].rearrange("p (h e) -> p h e", h=DH)
                step.then(TT(o, o, oss[0:m, r, :, None].broadcast_to([m, DH, EV]), ALU.mult))
                TT(o, o, d_gain[0:m, None, :].broadcast_to([m, DH, EV]), ALU.mult).then_inc(L["on3_ok"], 1)
            for r, (c0, m) in enumerate(RT):
                dve.wait_ge(L["on_hi"], NR + r + 1)
                for b in range(2):
                    k4 = slice(4 * b, 4 * b + 4)
                    ins = TT(h_lo[:, k4, c0:c0 + m], ps[:, b, 0:4 * m].rearrange("p (k t) -> p k t", k=4), f32(h_hi[:, k4, c0:c0 + m]),
                             ALU.subtract)
                ins.then_inc(L["on_lo"], 1)
            add_bias(gate, 1, 2)
            over("dout", stream_out("dout", 0))
            ffn(1)


_INS = ['x_prompt', 'x_sample', 'state_gla', 'cache_diff_k', 'cache_diff_v', 'state_ffn_conv', 'c_prompt', 'c_sample',
        'norm_mix', 'norm_ffn', 'w_ada', 'b_ada', 'gla_w_in', 'gla_w_alpha', 'gla_b_alpha', 'gla_norm', 'gla_w_out',
        'diff_w_in', 'diff_q_norm', 'diff_k_norm', 'diff_lambda', 'diff_norm', 'diff_w_out',
        'ffn_w_in', 'ffn_conv_w', 'ffn_conv_b', 'ffn_w_out']


def kernel(**inputs):
    import numpy as np
    from concourse import bacc
    from concourse.bass_utils import run_bass_kernel_spmd

    nc = bacc.Bacc("TRN2", target_bir_lowering=False, num_devices=1)
    arrays, aps = {}, {}
    for name in _INS:
        a = np.ascontiguousarray(inputs[name])
        arrays[f"in_{name}"] = a
        aps[name] = nc.dram_tensor(f"in_{name}", a.shape, mybir.dt.from_np(a.dtype), kind="ExternalInput").ap()
    xp, xs = inputs["x_prompt"].shape, inputs["x_sample"].shape
    sg, ck, cv = inputs["state_gla"].shape, inputs["cache_diff_k"].shape, inputs["cache_diff_v"].shape
    fc = inputs["state_ffn_conv"].shape
    shapes = [xp, xs, (sg[0], xp[0]) + sg[2:], sg,
              (ck[0], xp[0], xp[1]) + ck[3:], (ck[0], xs[0], xs[1]) + ck[3:],
              (cv[0], xp[0], xp[1]) + cv[3:], (cv[0], xs[0], xs[1]) + cv[3:],
              (fc[0], xp[0]) + fc[2:], fc]
    outs = [nc.dram_tensor(f"out_{i}", s, F32, kind="ExternalOutput").ap() for i, s in enumerate(shapes)]
    hybrid_stream_step(nc, aps, outs)
    r = run_bass_kernel_spmd(nc, [arrays], core_ids=[0])
    return tuple(r.results[0][f"out_{i}"] for i in range(len(shapes)))
```

```python
import math
from contextlib import ExitStack

import concourse.bass as bass
from concourse import mybir

F32 = mybir.dt.float32
F32R = mybir.dt.float32r
BF16 = mybir.dt.bfloat16
U32 = mybir.dt.uint32
ALU = mybir.AluOpType
ACT = mybir.ActivationFunctionType
AX_X = mybir.AxisListType.X

P = 128
EPS = 1e-6
TAU = 16.0
CHUNK = 64
BLOCK_COLS = 256


class Steps:

    def __init__(self, eng, sem):
        self.eng, self.sem, self.n, self.at = eng, sem, 0, 0

    def then(self, ins):
        self.n += 1
        ins.then_inc(self.sem, 1)
        self.eng.wait_ge(self.sem, self.at + self.n)

    def loop(self, i, per):
        self.base, self.per, self.start = self.at + self.n, per, self.n
        self.at, self.n = i * per + self.base, 0

    def end(self, count):
        assert self.n == self.per, (self.n, self.per)
        self.at, self.n = self.base + self.per * count, 0


def hybrid_stream_step(nc, A, O):
    D = A["x_prompt"].shape[2]
    TP, TS = A["x_prompt"].shape[1], A["x_sample"].shape[1]
    T = TP + TS
    KT = D // P
    RT = [(r * P, P) for r in range(TP // P)] + [(TP, TS)]
    NR = len(RT)
    NPR = TP // P
    HALF = T // 2
    PB = TP - HALF
    GH, DK, DV = A["state_gla"].shape[2:]
    RANK = A["gla_w_alpha"].shape[1]
    NQ, NV = GH * DK, GH * DV
    DEPTH, _, FF2 = A["ffn_w_in"].shape
    FF = FF2 // 2
    FT = FF // P
    PAST = A["cache_diff_k"].shape[2]
    NPAST = PAST // P
    DH, _, HD = A["cache_diff_k"].shape[3:]
    EV = 2 * HD
    SCALE = HD ** -0.5
    LAM_INIT = 0.8 - 0.6 * math.exp(-0.3)
    W = T + 2
    CH = [6, 6, 6, FT - 18]
    CMAX = max(CH)
    WB = KT * BLOCK_COLS
    ADA_TILES = 6 * KT
    assert WB // 4 == NQ and T % 4 == 0 and DK == P and EV == P and sum(CH) == FT and all(c % 2 == 0 for c in CH)

    order = [("ada0", 8), ("qk", 4), ("v", 4), ("r", 4), ("gout", 4)]
    ffn_order = [("up", 0), ("up", 1), ("down", 0), ("up", 2), ("down", 1), ("up", 3), ("down", 2), ("down", 3)]
    nblk = lambda kind, c: CH[c] if kind == "up" else D // BLOCK_COLS
    order += [((0, k, c), nblk(k, c)) for k, c in ffn_order]
    order += [("dq", 4), ("dk", 4), ("dv", 4), ("dout", 4)]
    order += [((1, k, c), nblk(k, c)) for k, c in ffn_order]
    BASE, n = {}, 0
    for name, k in order:
        BASE[name] = n
        n += k
    NBLOCKS = n
    ride, n = {}, 0
    RIDES = ["qk", "v", "r", "gout", (0, "up", 0), (0, "up", 1), (0, "up", 3), "dq", "dk"]
    for name in RIDES:
        ride[name] = n
        n += dict(order)[name]
    assert n == 2 * ADA_TILES // 2 - 8
    TILE, n = {}, 0
    tiles = [("qk", 8), ("alow", 1), ("gout", 8)]
    ffn_tiles = lambda l: [((l, k, c), 2 * nblk(k, c)) for k, c in ffn_order]
    tiles += ffn_tiles(0) + [("dout", 8)] + ffn_tiles(1)
    for name, k in tiles:
        TILE[name] = n
        n += k
    READ_BY_ACT = {n for n, _ in tiles if n in ("qk", "alow") or "up" in n}
    BEFORE_NORM = {1: "gout", 2: (0, "down", len(CH) - 1), 3: "dout"}
    AFTER_NORM = ["qk", (0, "up", 0), "dq", (1, "up", 0)]
    READ_A, READ_D, FIRST, a, dd, ff = {}, {}, {}, 1, 2, 0
    for name, k in tiles + [("end", 0)]:
        READ_A[name], READ_D[name], FIRST[name] = a, dd, ff
        if name in READ_BY_ACT:
            a += k
        else:
            dd += k
        ff += max(1, k // 2)
    ROWS, n = {}, 0
    for name in ["v", "r", "dq", "dk", "dv"]:
        ROWS[name] = n
        n += 4 * NR
    FIRST_ROWS = {name: k * (NR - 1) // NR for name, k in ROWS.items()}

    ctx = ExitStack()
    with ctx:
        def sb(name, shape, dt=F32, c=ctx):
            return c.enter_context(nc.sbuf_tensor(name, shape, dt))

        def sem(name):
            return ctx.enter_context(nc.semaphore(name))

        ps = ctx.enter_context(nc.psum_tensor("ps", [P, 8, 512], F32))
        bank = lambda b: ps[:, b, :]

        xT = sb("xT", [P, KT, T])
        h_hi = sb("h_hi", [P, KT, T], F32R)
        low = ExitStack()
        h_lo = sb("h_lo", [P, KT, T], F32R, c=low)
        low.close()
        second = sb("second", [P, KT, T])
        w_raw = sb("w_raw", [P, 2, WB])
        w_hi = sb("w_hi", [P, 2, WB], F32R)
        w_lo = sb("w_lo", [P, 2, WB], F32R)
        a_raw = sb("a_raw", [P, WB // 2])
        side = ExitStack()
        a_hi = sb("a_hi", [P, WB // 2], F32R, c=side)
        a_lo = sb("a_lo", [P, WB // 2], F32R, c=side)
        side.close()
        spare = sb("spare", [P, 4, WB // 4])
        ident = sb("ident", [P, P])
        ones = sb("ones", [P, P])
        cum = sb("cum", [P, P])
        low_rows = sb("low_rows", [1, P], BF16)
        neg_cols = sb("neg_cols", [1, P], BF16)
        eps = sb("eps", [P, 1])
        zero2 = sb("zero2", [P, 2])
        norm_g = sb("norm_g", [P, 4, KT])
        b_ada = sb("b_ada", [P, DEPTH, ADA_TILES])
        conv_c = sb("conv_c", [P, 6 * DEPTH, 2 * FT])
        ada = sb("ada", [P, DEPTH, ADA_TILES, 2])
        cs = sb("cs", [P, 2 * KT])
        c_st = sb("c_st", [P, KT, 32], F32R)
        ada_t = sb("ada_t", [32, BLOCK_COLS])
        gain = sb("gain", [P, KT, 2])
        shift = sb("shift", [P, KT, 2])
        gate = sb("gate", [P, KT, 2])
        new_conv = sb("new_conv", [P, 2 * FT, 4])
        stat = sb("stat", [P, 64])
        nc_rows = sb("nc_rows", [2 * FT, 4, P])

        pro = ExitStack()
        x_rows = sb("x_rows", [P, NR, D], c=pro)
        vec_rows = sb("vec_rows", [P, 3 + 6 * DEPTH, P], c=pro)
        pro.close()
        nrm = ExitStack()
        sq = sb("sq", [P, 2, T], c=nrm)
        rstd = sb("rstd", [P, T], c=nrm)
        nrm.close()
        g = ExitStack()
        qk = sb("qk", [P, 2 * GH, T], c=g)
        v_r = sb("v_r", [P, NR, NV], c=g)
        r_r = sb("r_r", [P, NR, NV], c=g)
        alT = sb("alT", [RANK + 1, T], c=g)
        w_alpha = sb("w_alpha", [RANK + 1, NQ], c=g)
        gla_g = sb("gla_g", [P, DV], c=g)
        tA = sb("tA", [P, NQ], c=g)
        tB = sb("tB", [P, NQ], c=g)
        tC = sb("tC", [P, NQ], c=g)
        qe = [sb("qe", [P, NQ], c=g), spare[:, 0, :]]
        kd_r = [sb("kd_r", [P, NQ], c=g), spare[:, 1, :]]
        att = [sb("att", [P, NQ], c=g), spare[:, 2, :]]
        g2 = ExitStack()
        aw = sb("aw", [P, KT, RANK], c=g2)
        aw_hi = sb("aw_hi", [P, KT, RANK], F32R, c=g2)
        aw_lo = sb("aw_lo", [P, KT, RANK], F32R, c=g2)
        g2.close()
        S = sb("S", [P, 3, GH, DV], c=g)
        dec = sb("dec", [P, GH, 2], c=g)
        g.close()
        f = ExitStack()
        act_hi = sb("act_hi", [P, 2, CMAX, W], F32R, c=f)
        act_lo = sb("act_lo", [P, 2, CMAX, W], F32R, c=f)
        up = sb("up", [P, 2, W + 2], c=f)
        cv1 = sb("cv1", [P, 2, W], c=f)
        cv = sb("cv", [P, 2, 2, W], c=f)
        f.close()
        d = ExitStack()
        q_r = sb("q_r", [P, NR, D], c=d)
        k_r = sb("k_r", [P, NR, D], c=d)
        vd_r = sb("vd_r", [P, NR, D], c=d)
        d2 = ExitStack()
        ssq = sb("ssq", [P, 2 * BLOCK_COLS], c=d2)
        lam_in = sb("lam_in", [P, 4, HD], c=d2)
        d2.close()
        qn = sb("qn", [P, NR, EV], c=d)
        kn = sb("kn", [P, NR, EV], c=d)
        kc, vc = (a_raw[:, n:n + PAST].rearrange("p (r e) -> p r e", e=EV) for n in (0, PAST))
        qT = [sb("qT", [P, T], c=d), second[:, 0, :]]
        kT = [sb("kT", [P, T], c=d), second[:, 1, :]]
        kcT = [sb("kcT", [P, PAST], c=d), second[:, 2, 0:PAST]]
        pr = sb("pr", [P, 2, 2, PAST + TS], c=d)
        aT = sb("aT", [P, PAST], c=d)
        q_gain = sb("q_gain", [P, HD], c=d)
        k_gain = sb("k_gain", [P, HD], c=d)
        d_gain = sb("d_gain", [EV, 1], c=d)
        ss = sb("ss", [P, NR, 2, 2 * DH], c=d)
        rs = sb("rs", [P, NR, 2, 2 * DH], c=d)
        osq = sb("osq", [P, EV], c=d)
        vs = sb("vs", [P, EV], c=d)
        oss = sb("oss", [P, NR, DH], c=d)
        ors = sb("ors", [P, NR, DH], c=d)
        d.close()
        e = ExitStack()
        y_rows = sb("y_rows", [P, 2, D], c=e)
        e.close()

        const_in = sem("const_in")
        vec_in = sem("vec_in")
        consts = sem("consts")
        ident_zero = sem("ident_zero")
        w_in = [sem("w_in0"), sem("w_in1")]
        w_hi_ok = sem("w_hi_ok")
        w_lo_ok = sem("w_lo_ok")
        w_used = sem("w_used")
        a_in = sem("a_in")
        a_hi_ok = sem("a_hi_ok")
        a_lo_ok = sem("a_lo_ok")
        a_used = sem("a_used")
        ada_done = sem("ada_done")
        ada_free = sem("ada_free")
        tile_done = sem("tile_done")
        tile_read_a = sem("tile_read_a")
        tile_read_d = sem("tile_read_d")
        rows_done = sem("rows_done")
        rows_free = sem("rows_free")
        dve_step = sem("dve_step")
        act_step = sem("act_step")
        turned = sem("turned")
        turned_out = sem("turned_out")
        c_hi_ok = sem("c_hi_ok")
        c_st_ok = sem("c_st_ok")
        x_loaded = sem("x_loaded")
        sq_ok = sem("sq_ok")
        sq_used = sem("sq_used")
        sums_done = sem("sums_done")
        root_ok = sem("root_ok")
        rms_used = sem("rms_used")
        xs_ok = sem("xs_ok")
        h_hi_ok = sem("h_hi_ok")
        h_ok = sem("h_ok")
        mod_ok = sem("mod_ok")
        up_ok = sem("up_ok")
        conv_ok = sem("conv_ok")
        silu_ok = sem("silu_ok")
        prod_ok = sem("prod_ok")
        act_hi_ok = sem("act_hi_ok")
        act_ok = sem("act_ok")
        state_out = sem("state_out")
        v_out = sem("v_out")
        phase_in = sem("phase_in")

        L = {}
        for name in ["al_ok", "aw_hi_ok", "aw_ok", "logit_ok", "logit_out", "g_ok", "b_ok", "b_sb_ok", "bd_ok", "exp_ok", "qe_ok",
                     "kd_turned", "kd_out", "attn_ok", "attn_out", "u_ok", "s1_ok", "s2_ok", "o_ok", "oss_ok", "on_ok",
                     "on_turned", "on_hi", "on_lo", "s_zero",
                     "ssq_ok", "ssq_used", "qkv_ok", "rs_ok", "qn_ok", "qn_gained", "head_turned", "head_outA", "head_outD",
                     "sc_ok", "mx_ok", "p_ok", "a_ok", "a_turned", "a_out", "av_ok", "av_out", "osq_ok", "kc_in", "kc_in2",
                     "kn_out", "on2_ok", "on3_ok", "fin_turned", "fin_out", "fin_stored0", "fin_stored1", "nc_turned", "nc_out", "nc_stored",
                     "lam_ok", "lsp_ok", "oss_raw", "s_in", "dg_ok", "vs_ok"]:
            L[name] = sem(name)

        ada_w = A["w_ada"].rearrange("l (k p) e -> l p k e", p=P)
        gla_w = A["gla_w_in"][0].rearrange("(k p) e -> p k e", p=P)
        gla_o = A["gla_w_out"][0].rearrange("(k p) e -> p k e", p=P)
        dif_w = A["diff_w_in"][0].rearrange("(k p) e -> p k e", p=P)
        dif_o = A["diff_w_out"][0].rearrange("(k p) e -> p k e", p=P)
        ffn_i = A["ffn_w_in"].rearrange("l (k p) e -> l p k e", p=P)
        ffn_o = A["ffn_w_out"].rearrange("l (k p) e -> l p k e", p=P)
        blk = lambda t, s, kt=KT: t[:, s, 0:kt * BLOCK_COLS].rearrange("p (k c) -> p k c", k=kt)
        ablk = lambda t: t[:, :].rearrange("p (k c) -> p k c", k=KT // 2)
        slot = lambda t, h, n=HALF, m=P: ps[0:m, 2 * (t % 2) + h, 0:n]

        def shared_ride(name, l=None):
            r = ride.get(name)
            if r is None:
                return None
            return (0, r + 8) if r < ADA_TILES // 2 - 8 else (1, r - (ADA_TILES // 2 - 8))

        UNITS = [NPR] + list(range(NPR))
        assert NR % 2 == 1 and DH % 2 == 0

        def unit(h, u):
            i, j = h
            j, u = j + u // NR, u % NR
            return 2 * i + j, u, (2 * i + j) * NR + u, (j + u) % 2

        beyond = lambda h: isinstance(h, int) and h >= DH

        block = ctx.enter_context(nc.Block())

        @block.sync
        def _(sp):
            sp.dma_start(x_rows[:, 0:NPR, :], A["x_prompt"][0].rearrange("(r p) d -> p r d", p=P)).then_inc(const_in, 16)
            sp.dma_start(x_rows[0:TS, NPR, :], A["x_sample"][0]).then_inc(const_in, 16)
            tiled = lambda ap: ap.rearrange("(k p) -> k p", p=P)
            sp.dma_start(vec_rows[0:KT, 0, :], tiled(A["c_prompt"][0])).then_inc(vec_in, 16)
            sp.dma_start(vec_rows[KT:2 * KT, 0, :], tiled(A["c_sample"][0])).then_inc(vec_in, 16)
            sp.dma_start(vec_rows[0:2 * KT, 1, :], A["norm_mix"].rearrange("l (k p) -> (l k) p", p=P)).then_inc(vec_in, 16)
            sp.dma_start(vec_rows[2 * KT:4 * KT, 1, :], A["norm_ffn"].rearrange("l (k p) -> (l k) p", p=P)).then_inc(vec_in, 16)
            sp.dma_start(vec_rows[0:DEPTH * ADA_TILES, 2, :], A["b_ada"].rearrange("l (k p) -> (l k) p", p=P)).then_inc(vec_in, 16)
            for l in range(DEPTH):
                sp.dma_start(vec_rows[0:2 * FT, 3 + 6 * l:6 + 6 * l, :],
                             A["ffn_conv_w"][l].rearrange("j (k p) -> k j p", p=P)).then_inc(vec_in, 16)
                sp.dma_start(vec_rows[0:2 * FT, 6 + 6 * l, :], tiled(A["ffn_conv_b"][l])).then_inc(vec_in, 16)
                sp.dma_start(vec_rows[0:2 * FT, 7 + 6 * l:9 + 6 * l, :],
                             A["state_ffn_conv"][l, 0].rearrange("j (k p) -> k j p", p=P)).then_inc(vec_in, 16)

            def load(n0, i, src, kt=KT):
                for j in range(2):
                    n = n0 + 2 * i + j
                    if not (isinstance(i, int) and n < 2):
                        sp.wait_ge(w_lo_ok, n - 1)
                    sp.dma_start(blk(w_raw, j, kt), src(i, j)).then_inc(w_in[j], 16)

            def phase(name, src, kt=KT, peel=False):
                pairs = dict(order)[name] // 2
                if peel:
                    load(BASE[name], 0, src, kt)
                with sp.Fori(1 if peel else 0, pairs) as i:
                    load(BASE[name], i, src, kt)

            col = lambda w, c0: (lambda i, j: w[:, :, bass.ds(c0 + (2 * i + j) * BLOCK_COLS, BLOCK_COLS)])

            phase("ada0", col(ada_w[0], 0), peel=True)
            phase("qk", col(gla_w, 0))
            sp.wait_ge(x_loaded, KT - 1)
            sp.dma_start(aw[:, :, :], gla_w[:, :, 2 * NQ + 2 * NV:2 * NQ + 2 * NV + RANK]).then_inc(phase_in, 16)
            sp.dma_start(w_alpha[0:RANK, :], A["gla_w_alpha"][0]).then_inc(phase_in, 16)
            sp.dma_start(w_alpha[RANK:RANK + 1, :], A["gla_b_alpha"]).then_inc(phase_in, 16)
            sp.dma_start(gla_g[:, :], A["gla_norm"][0].partition_broadcast(P)).then_inc(phase_in, 16)
            phase("v", col(gla_w, 2 * NQ))
            phase("r", col(gla_w, 2 * NQ + NV))
            phase("gout", col(gla_o, 0))

            def ffn_loads(l):
                for kind, c in ffn_order:
                    c0 = sum(CH[:c])
                    if kind == "up":
                        phase((l, kind, c), lambda i, j, c0=c0: ffn_i[l][:, :, bass.ds(j * FF + (c0 + 2 * i) * P, BLOCK_COLS)])
                    else:
                        phase((l, kind, c), col(ffn_o[l][:, c0:c0 + CH[c], :], 0), kt=CH[c])

            ffn_loads(0)
            phase("dq", col(dif_w, 0))
            sp.wait_ge(w_used, BASE["dq"])
            bc = lambda ap: ap.partition_broadcast(P)
            sp.dma_start(q_gain[:, :], bc(A["diff_q_norm"][0])).then_inc(phase_in, 16)
            sp.dma_start(k_gain[:, :], bc(A["diff_k_norm"][0])).then_inc(phase_in, 16)
            sp.dma_start(d_gain[:, :], A["diff_norm"][0].rearrange("(e a) -> e a", a=1)).then_inc(phase_in, 16)
            sp.dma_start(lam_in[:, :, :], bc(A["diff_lambda"][0])).then_inc(phase_in, 16)
            phase("dk", col(dif_w, D))
            phase("dv", col(dif_w, 2 * D))
            load(BASE["dout"], 0, col(dif_o, 0))
            sp.wait_ge(rows_free, ROWS["dv"] + 4 * NR + 2)
            ov = [O[6][0, 0].rearrange("t h e -> t (h e)"), O[7][0, 0].rearrange("t h e -> t (h e)")]
            sp.dma_start(ov[0].rearrange("(r p) e -> p r e", p=P), vd_r[:, 0:NPR, :]).then_inc(v_out, 16)
            sp.dma_start(ov[1], vd_r[0:TS, NPR, :]).then_inc(v_out, 16)
            ck = A["cache_diff_k"][0, 0].rearrange("(r p) h s d -> p r (h s d)", p=P)
            cvv = A["cache_diff_v"][0, 0].rearrange("(r p) h e -> p r (h e)", p=P)
            ok0 = O[4][0, 0].rearrange("(r p) h s d -> p r (h s d)", p=P)
            ok1 = O[5][0, 0].rearrange("t h s d -> t (h s d)")
            sp.wait_ge(a_lo_ok, 4 * (ADA_TILES // 2) - 16)

            def head_io(h):
                if not isinstance(h, int):
                    sp.wait_ge(L["head_turned"], 2 * h)
                sp.dma_start(kc[:, :, :], ck[:, :, bass.ds(h * EV, EV)]).then_inc(L["kc_in"], 16)
                sp.wait_ge(L["qn_gained"], h + 1)
                sp.dma_start(ok0[:, :, bass.ds(h * EV, EV)], kn[:, 0:NPR, :]).then_inc(L["kn_out"], 16)
                sp.dma_start(ok1[:, bass.ds(h * EV, EV)], kn[0:TS, NPR, :]).then_inc(L["kn_out"], 16)
                if not isinstance(h, int):
                    sp.wait_ge(L["av_ok"], h * NR - NR + 1)
                sp.dma_start(vc[:, :, :], cvv[:, :, bass.ds(h * EV, EV)]).then_inc(L["kc_in2"], 16)

            head_io(0)
            with sp.Fori(1, DH) as h:
                head_io(h)
            load(BASE["dout"], 1, col(dif_o, 0))
            ffn_loads(1)

            for r, (c0, m) in enumerate(RT):
                sp.wait_ge(L["fin_out"], r + 1)
                dst = O[0][0, c0:c0 + m, :] if r < NPR else O[1][0]
                sp.dma_start(dst, y_rows[0:m, r % 2, :]).then_inc(L["fin_stored%d" % (r % 2)], 16)
            sp.wait_ge(L["fin_stored0"], 16 * ((NR + 1) // 2))
            sp.wait_ge(L["fin_stored1"], 16 * (NR // 2))
            sp.wait_ge(L["kn_out"], 32 * DH)
            sp.wait_ge(L["nc_stored"], 64 * DEPTH)
            sp.wait_ge(v_out, 32)
            sp.wait_ge(state_out, 32)

        @block.gpsimd
        def _(pool):
            pool.memset(ident[:, :], 0.0).then_inc(ident_zero, 1)
            pool.memset(ones[:, :], 1.0).then_inc(ident_zero, 1)
            pool.memset(cum[:, :], 0.0).then_inc(ident_zero, 1)
            pool.memset(low_rows[:, :], 0.0).then_inc(ident_zero, 1)
            pool.memset(neg_cols[:, :], 0.0).then_inc(ident_zero, 1)
            pool.wait_ge(ident_zero, 5)
            pool.affine_select(out=ident[:, :], in_=ident[:, :], compare_op=ALU.not_equal, fill=1.0, base=0,
                               pattern=[[-1, P]], channel_multiplier=1).then_inc(consts, 1)
            pool.memset(eps[:, :], EPS).then_inc(consts, 1)
            pool.memset(zero2[:, :], 0.0).then_inc(consts, 1)
            pool.memset(low_rows[:, 0:CHUNK], 1.0).then_inc(consts, 1)
            pool.memset(neg_cols[:, CHUNK:P], -1e30).then_inc(consts, 1)
            for c in range(P // CHUNK):
                s = slice(c * CHUNK, (c + 1) * CHUNK)
                pool.memset(cum[s, s], 1.0 / TAU).then_inc(ident_zero, 1)
                pool.wait_ge(ident_zero, 6 + c)
                pool.affine_select(out=cum[s, s], in_=cum[s, s], compare_op=ALU.is_ge, fill=0.0, base=0,
                                   pattern=[[1, CHUNK]], channel_multiplier=-1).then_inc(consts, 1)
            def ada_loads(name):
                l, b0 = shared_ride(name)

                def pair(i):
                    for j in range(2):
                        for half in range(2):
                            a = 2 * (ride[name] + 2 * i + j) + half
                            if not (isinstance(i, int) and a < 1):
                                pool.wait_ge(a_lo_ok, a)
                            pool.dma_start(ablk(a_raw), ada_w[l][:, half * KT // 2:(half + 1) * KT // 2,
                                                                 bass.ds((b0 + 2 * i + j) * BLOCK_COLS, BLOCK_COLS)]).then_inc(a_in, 16)

                if ride[name] == 0:
                    pair(0)
                with pool.Fori(1 if ride[name] == 0 else 0, dict(order)[name] // 2) as i:
                    pair(i)

            for name in ("qk", "v", "r"):
                ada_loads(name)
            pool.wait_ge(L["o_ok"], NPR)
            pool.dma_start(S[:, (2 * NPR + 1) % 3], A["state_gla"][0, 0].rearrange("h d e -> d h e")).then_inc(L["s_in"], 16)
            pool.wait_ge(L["s2_ok"], NPR)
            pool.dma_start(O[2][0, 0].rearrange("h d e -> d h e"), S[:, (2 * NPR) % 3]).then_inc(state_out, 16)
            pool.wait_ge(L["s2_ok"], NPR + 1)
            pool.dma_start(O[3][0, 0].rearrange("h d e -> d h e"), S[:, (2 * NPR + 2) % 3]).then_inc(state_out, 16)
            for name in RIDES[3:]:
                ada_loads(name)
            grp = lambda t: t[:, :, :].rearrange("p r (s d) -> p (r s) d", d=HD)
            g_of = lambda t: t[:, None, :].broadcast_to([P, 2 * NR, HD])
            pool.wait_ge(phase_in, 128)
            pool.wait_ge(rows_free, ROWS["dv"] + 4 * NR + 2)

            def head_gains(h):
                pool.wait_ge(L["qn_ok"], h + 1)
                pool.tensor_tensor(grp(qn), grp(qn), g_of(q_gain), ALU.mult)
                pool.tensor_tensor(grp(kn), grp(kn), g_of(k_gain), ALU.mult).then_inc(L["qn_gained"], 1)
                if not isinstance(h, int):
                    pool.wait_ge(L["av_ok"], h * NR - NR + 1)
                pool.tensor_copy(vs[0:TS, :], vd_r[0:TS, NPR, bass.ds(h * EV, EV)]).then_inc(L["vs_ok"], 1)

            head_gains(0)
            with pool.Fori(1, DH) as h:
                head_gains(h)

            for l in range(DEPTH):
                pool.wait_ge(L["nc_out"], l + 1)
                for gs in range(4):
                    dst = O[8 + gs // 2][l, 0, gs % 2].rearrange("(k p) -> k p", p=P)
                    pool.dma_start(dst, nc_rows[:, gs, :]).then_inc(L["nc_stored"], 16)

        @block.tensor
        def _(pe):
            def products(out, lhs_hi, lhs_lo, rhs_hi, rhs_lo, first, last):
                for part in range(len(out)):
                    pe.matmul(out[part], lhs_hi, rhs_hi[part], start=first, stop=False)
                    pe.matmul(out[part], lhs_hi, rhs_lo[part], start=False, stop=False)
                for part in range(len(out)):
                    ins = pe.matmul(out[part], lhs_lo, rhs_hi[part], start=False, stop=last)
                return ins

            h_parts = lambda t, k: [t[:, k, 0:HALF], t[:, k, HALF:T]]

            def rider(name, i, j, half):
                if name in ride:
                    a = ride[name] + 2 * i + j
                    pe.wait_ge(a_lo_ok, 2 * a + half + 1)
                    if half == 0:
                        pe.wait_ge(ada_free, a + 8)
                    out = ps[0:32, 7, 0:BLOCK_COLS]
                    for k in range(KT // 2):
                        c = c_st[:, half * KT // 2 + k, :]
                        pe.matmul(out, c, ablk(a_hi)[:, k, :], start=(half == 0 and k == 0), stop=False)
                        ins = pe.matmul(out, c, ablk(a_lo)[:, k, :], start=False, stop=(half == 1 and k == KT // 2 - 1))
                    ins.then_inc(ada_done, 1)

            def before(name, but=0):
                names = [n for n, _ in tiles]
                last = names[names.index(name) - 1] if name != names[0] else None
                n_a = READ_A[name] - but * (last in READ_BY_ACT)
                n_d = READ_D[name] - but * (last not in READ_BY_ACT)
                if n_a > 1:
                    pe.wait_ge(tile_read_a, n_a)
                if n_d > 2:
                    pe.wait_ge(tile_read_d, n_d)

            def columns(name, parts_hi, parts_lo, kt=KT, widths=(HALF, HALF), after=None, squares=None):
                before(name, but=1)

                def pair(i):
                    for j in range(2):
                        pe.wait_ge(w_lo_ok, BASE[name] + 2 * i + j + 1)
                        for t in range(2):
                            if j == 0 and t == 1:
                                before(name)
                            if name in READ_BY_ACT:
                                wait, n = tile_read_a, READ_A[name] + 4 * i + 2 * j + t - 1
                            else:
                                wait, n = tile_read_d, READ_D[name] + 4 * i + 2 * j + t - 1
                            if not (isinstance(n, int) and n < 1):
                                pe.wait_ge(wait, n)
                            s = (TILE[name] + 2 * j + t) % 2
                            out = [ps[:, 2 * s, 0:widths[0]], ps[:, 2 * s + 1, 0:widths[1]]]
                            for k in range(kt):
                                if after is not None and isinstance(i, int) and j == t == 0:
                                    pe.wait_ge(h_ok, after * KT + k + 1)
                                c = slice(t * P, (t + 1) * P)
                                ins = products(out, blk(w_hi, j, kt)[:, k, c], blk(w_lo, j, kt)[:, k, c],
                                               parts_hi(k), parts_lo(k), k == 0, k == kt - 1)
                            ins.then_inc(w_used if t else tile_done, 1)
                            rider(name, i, j, t)
                            if squares and 4 * i + 2 * j + t:
                                sum_squares(squares, 4 * i + 2 * j + t - 1)

                phase(name, pair, after is not None, squares)
                if squares:
                    sum_squares(squares, KT - 1)

            def phase(name, pair, peel=False, unroll=False):
                pairs = dict(order)[name] // 2
                straight = pairs if unroll else int(peel)
                for i in range(straight):
                    pair(i)
                if straight < pairs:
                    with pe.Fori(straight, pairs) as i:
                        pair(i)

            def rows(name, after=None):
                def pair(i):
                    for j in range(2):
                        pe.wait_ge(w_lo_ok, BASE[name] + 2 * i + j + 1)
                        for r, (c0, m) in enumerate(RT):
                            n = ROWS[name] + 2 * NR * i + NR * j + r
                            pe.wait_ge(rows_free, n + 1)
                            b = 4 + (NR * j + r) % 2
                            out = ps[0:m, b, 0:BLOCK_COLS]
                            for k in range(KT):
                                if after is not None and isinstance(i, int) and j == r == 0:
                                    pe.wait_ge(h_ok, after * KT + k + 1)
                                hh, hl = h_hi[:, k, c0:c0 + m], h_lo[:, k, c0:c0 + m]
                                wh, wl = blk(w_hi, j)[:, k, :], blk(w_lo, j)[:, k, :]
                                pe.matmul(out, hh, wh, start=(k == 0), stop=False)
                                pe.matmul(out, hh, wl, start=False, stop=False)
                                ins = pe.matmul(out, hl, wh, start=False, stop=(k == KT - 1))
                            ins.then_inc(w_used if r == NR - 1 else rows_done, 1)
                            if r in (1, NR - 1):
                                rider(name, i, j, int(r > 1))

                phase(name, pair, after is not None)

            def sum_squares(which, k):
                pe.wait_ge(sq_ok, which * KT + k + 1)
                pe.matmul(ps[:, 4, 0:HALF], ones[:, :], sq[:, k % 2, 0:HALF], start=(k == 0), stop=(k == KT - 1))
                pe.matmul(ps[:, 5, 0:HALF], ones[:, :], sq[:, k % 2, HALF:T], start=(k == 0), stop=(k == KT - 1)) \
                  .then_inc(sq_used if k < KT - 1 else sums_done, 1)

            pe.wait_ge(consts, 7)
            pe.wait_ge(vec_in, 16 * (5 + 3 * DEPTH))
            sizes = [2 * KT, 4 * KT, DEPTH * ADA_TILES] + [2 * FT] * (6 * DEPTH)
            for v, m in enumerate(sizes):
                ins = pe.transpose(ps[:, v // 4, (v % 4) * P:(v % 4) * P + m], vec_rows[0:m, v, :], ident[0:m, 0:m])
            ins.then_inc(turned, 1)
            pe.wait_ge(const_in, 32)
            for k in range(KT):
                if k >= 2:
                    pe.wait_ge(x_loaded, k - 1)
                for r in range(NPR):
                    ins = pe.transpose(ps[:, 4 + k % 2, r * P:(r + 1) * P], x_rows[:, r, k * P:(k + 1) * P], ident[:, :])
                ins = pe.transpose(ps[:, 6, k * TS:(k + 1) * TS], x_rows[0:TS, NPR, k * P:(k + 1) * P], ident[0:TS, 0:TS])
                ins.then_inc(turned, 1)

            for k in range(KT):
                sum_squares(0, k)

            pe.sem_inc(ada_done, 1)
            pe.wait_ge(c_st_ok, 1)

            def ada_main(i):
                for j in range(2):
                    n = 2 * i + j
                    pe.wait_ge(w_lo_ok, n + 1)
                    if not (isinstance(n, int) and n < 1):
                        pe.wait_ge(ada_free, n)
                    out = ps[0:32, 7, 0:BLOCK_COLS]
                    for k in range(KT):
                        pe.matmul(out, c_st[:, k, :], blk(w_hi, j)[:, k, :], start=(k == 0), stop=False)
                        ins = pe.matmul(out, c_st[:, k, :], blk(w_lo, j)[:, k, :], start=False, stop=(k == KT - 1))
                    ins.then_inc(w_used, 1)

            ada_main(0)
            with pe.Fori(1, 4) as i:
                ada_main(i)

            pe.wait_ge(turned_out, 1)
            columns("qk", lambda k: h_parts(h_hi, k), lambda k: h_parts(h_lo, k), after=0)
            t = TILE["alow"]
            pe.wait_ge(L["aw_ok"], 1)
            before("alow")
            for k in range(KT):
                ins = products([slot(t, 0, m=RANK), slot(t, 1, m=RANK)], aw_hi[:, k, :], aw_lo[:, k, :],
                               h_parts(h_hi, k), h_parts(h_lo, k), k == 0, k == KT - 1)
            ins.then_inc(tile_done, 1)
            pe.wait_ge(x_loaded, KT - 1)
            rows("v")
            rows("r")

            before("gout")
            pe.wait_ge(rows_free, ROWS["dq"] + 2)
            pe.wait_ge(ada_free, ride["gout"] + 8)

            def logits(r):
                if r < NR:
                    c0, m = RT[r]
                    if r:
                        pe.wait_ge(L["attn_out"], r)
                    pe.matmul(ps[0:m, 7, :], alT[:, c0:c0 + m], w_alpha[:, :], start=True, stop=True).then_inc(L["logit_ok"], 1)

            def running_sums(r):
                if r < NR:
                    m = RT[r][1]
                    pe.wait_ge(L["g_ok"], r + 1)
                    for h in range(GH):
                        ins = pe.matmul(ps[:, 7, h * m:(h + 1) * m], tA[0:m, h * P:(h + 1) * P], cum[0:m, 0:m], start=True, stop=True)
                    ins.then_inc(L["b_ok"], 1)

            def keys_and_scores(r):
                if r < NR:
                    m = RT[r][1]
                    pe.wait_ge(L["qe_ok"], r + 1)
                    if r:
                        pe.wait_ge(L["kd_out"], r)
                    for h in range(GH):
                        ins = pe.transpose(ps[0:m, 0, h * P:(h + 1) * P], tC[:, h * m:(h + 1) * m], ident[:, :])
                    ins.then_inc(L["kd_turned"], 1)
                    for h in range(GH):
                        ins = pe.matmul(ps[0:m, 7, h * m:(h + 1) * m], tB[:, h * m:(h + 1) * m], qe[r % 2][:, h * m:(h + 1) * m],
                                        start=True, stop=True)
                    ins.then_inc(L["attn_ok"], 1)

            logits(0)
            running_sums(0)
            keys_and_scores(0)
            for r, (c0, m) in enumerate(RT):
                nch = max(1, m // CHUNK)
                C = m // nch
                logits(r + 1)
                pe.wait_ge(L["kd_out"], r + 1)
                if r:
                    pe.wait_ge(L["s2_ok"], r)
                for c in range(nch):
                    for h in range(GH):
                        b = [[1, 2], [3, 5]][c][h // 2]
                        ins = pe.matmul(ps[:, b, (h % 2) * DV:(h % 2 + 1) * DV], kd_r[r % 2][c * C:(c + 1) * C, h * P:(h + 1) * P],
                                        v_r[c * C:(c + 1) * C, r, h * DV:(h + 1) * DV], start=True, stop=True)
                ins.then_inc(L["u_ok"], 1)
                running_sums(r + 1)
                pe.wait_ge(L["attn_out"], r + 1)
                pe.wait_ge(L["s1_ok"], r + 1)
                if r == 0:
                    pe.wait_ge(L["s_zero"], 1)
                else:
                    pe.wait_ge(L["on_lo"], r)
                s0 = 2 * r if r < NPR else 2 * NPR + 1
                for h in range(GH):
                    b = [4, 6][h // 2]
                    o = slice((h % 2) * DV, (h % 2 + 1) * DV)
                    pe.matmul(ps[0:m, b, o], att[r % 2][0:m, h * m:(h + 1) * m], v_r[0:m, r, h * DV:(h + 1) * DV],
                              start=True, stop=False, skip_group_check=True)
                    for c in range(nch):
                        ins = pe.matmul(ps[c * C:(c + 1) * C, b, o], qe[r % 2][:, h * m + c * C:h * m + (c + 1) * C],
                                        S[:, (s0 + c) % 3, h, :], start=False, stop=(c == nch - 1), skip_group_check=True)
                ins.then_inc(L["o_ok"], 1)
                keys_and_scores(r + 1)
                pe.wait_ge(L["on_ok"], r + 1)
                for k in range(KT):
                    ins = pe.transpose(ps[:, [4, 6][k // 4], (k % 4) * m:(k % 4 + 1) * m], r_r[0:m, r, k * P:(k + 1) * P], ident[0:m, 0:m])
                ins.then_inc(L["on_turned"], 1)
            pe.wait_ge(L["on_lo"], NR)
            columns("gout", lambda k: h_parts(h_hi, k), lambda k: h_parts(h_lo, k), squares=1)

            def ffn(l):
                for kind, c in ffn_order:
                    if kind == "up":
                        columns((l, kind, c), lambda k: h_parts(h_hi, k), lambda k: h_parts(h_lo, k),
                                after=None if c else 2 * l + 1)
                    else:
                        pe.wait_ge(act_ok, l * FT + sum(CH[:c + 1]))
                        cp = lambda t: (lambda k: [t[:, c % 2, k, 0:HALF], t[:, c % 2, k, HALF:W]])
                        columns((l, kind, c), cp(act_hi), cp(act_lo), kt=CH[c], widths=(HALF, W - HALF),
                                squares=2 if BEFORE_NORM[2] == (l, kind, c) else None)
                if l:
                    pe.wait_ge(L["nc_out"], l)
                for gs in range(4):
                    ins = pe.transpose(ps[0:2 * FT, 6, gs * P:(gs + 1) * P], new_conv[:, :, gs], ident[:, :])
                ins.then_inc(L["nc_turned"], 1)

            ffn(0)

            for name in ("dq", "dk", "dv"):
                rows(name, after=2 if name == "dq" else None)
            pe.wait_ge(rows_free, ROWS["dv"] + 4 * NR + 2)

            def turn_head(h, part):
                if part == 0:
                    pe.wait_ge(L["qn_gained"], h + 1)
                    if not (isinstance(h, int) and h == 0):
                        pe.wait_ge(L["p_ok"], h * NR - NR + 1)
                    for r in range(NPR):
                        pe.transpose(ps[:, 2, r * P:(r + 1) * P], qn[:, r, :], ident[:, :])
                        ins = pe.transpose(ps[:, 3, r * P:(r + 1) * P], kn[:, r, :], ident[:, :])
                else:
                    pe.wait_ge(L["kc_in"], 16 * h + 16)
                    pe.wait_ge(L["head_outA"], 2 * h + 1)
                    pe.wait_ge(L["head_outD"], 2 * h + 1)
                    for r in range(NPAST):
                        pe.transpose(ps[:, 2, r * P:(r + 1) * P], kc[:, r, :], ident[:, :])
                    pe.transpose(ps[:, 3, 0:TS], qn[0:TS, NPR, :], ident[0:TS, 0:TS])
                    ins = pe.transpose(ps[:, 3, TS:2 * TS], kn[0:TS, NPR, :], ident[0:TS, 0:TS])
                ins.then_inc(L["head_turned"], 1)

            def scores_free(at, ahead):
                h, u, n, s = unit(at, ahead)
                if beyond(h):
                    return
                if u == 0:
                    pe.wait_ge(L["head_outA"], 2 * h + 2)
                    pe.wait_ge(L["head_outD"], 2 * h + 2)
                if not (isinstance(n, int) and n < 2):
                    pe.wait_ge(L["p_ok"], n - 1)

            def scores(at, ahead):
                h, u, n, s = unit(at, ahead)
                if beyond(h):
                    return
                r = UNITS[u]
                c0, m = RT[r]
                b = 4 + 2 * s
                if u:
                    scores_free(at, ahead)
                hp = (at[1] + (ahead // NR)) % 2
                for c in range(2):
                    e = slice(c * HD, (c + 1) * HD)
                    q = qT[hp][e, c0:c0 + m]
                    if r < NPR:
                        nk = (r + 1) * P
                        pe.matmul(ps[:, b + c, nk - P:nk], low_rows[:, :], neg_cols[:, :], start=True, stop=False,
                                  skip_group_check=True)
                        ins = pe.matmul(ps[:, b + c, 0:nk], q, kT[hp][e, 0:nk], start=False, stop=True, skip_group_check=True)
                    else:
                        pe.matmul(ps[0:m, b + c, 0:PAST], q, kcT[hp][e, :], start=True, stop=True)
                        ins = pe.matmul(ps[0:m, 2 + c, 0:TS], q, kT[hp][e, TP:T], start=True, stop=True)
                ins.then_inc(L["sc_ok"], 1)

            key_blocks = lambda r: r + 1 if r < NPR else NPAST + 1

            def weights_ready(at, ahead):
                h, u, n, s = unit(at, ahead)
                if not beyond(h):
                    pe.wait_ge(L["a_ok"], n + 1)

            def turn_weights(at, ahead):
                h, u, n, s = unit(at, ahead)
                if beyond(h):
                    return
                r = UNITS[u]
                m = RT[r][1]
                for b in range(key_blocks(r)):
                    kw = TS if r == NPR and b == NPAST else P
                    ins = pe.transpose(ps[0:kw, 0, b * m:(b + 1) * m], pr[0:m, s, 0, b * P:b * P + kw], ident[0:m, 0:m])
                ins.then_inc(L["a_turned"], 1)

            def values(at, ahead):
                h, u, n, s = unit(at, ahead)
                r = UNITS[u]
                m = RT[r][1]
                pe.wait_ge(L["a_out"], n + 1)
                pe.wait_ge(L["av_out"], n + 1)
                if u == 0:
                    pe.wait_ge(L["kc_in2"], 16 * h + 16)
                    pe.wait_ge(L["vs_ok"], h + 1)
                nb = key_blocks(r)
                for b in range(nb):
                    if r < NPR:
                        lhs, rhs = aT[:, b * m:(b + 1) * m], vd_r[:, b, bass.ds(h * EV, EV)]
                    elif b < NPAST:
                        lhs, rhs = aT[:, b * m:(b + 1) * m], vc[:, b, :]
                    else:
                        lhs, rhs = aT[0:TS, b * m:(b + 1) * m], vs[0:TS, :]
                    ins = pe.matmul(ps[0:m, 1, 0:EV], lhs, rhs, start=(b == 0), stop=(b == nb - 1))
                ins.then_inc(L["av_ok"], 1)

            turn_head(0, 0)
            turn_head(0, 1)
            scores_free((0, 0), 0)
            for u in range(3):
                scores((0, 0), u)
            weights_ready((0, 0), 0)
            turn_weights((0, 0), 0)
            def two_heads(i):
                for j in range(2):
                    for u in range(NR):
                        if (u + 3) % NR == 0:
                            scores_free((i, j), u + 3)
                        values((i, j), u)
                        if u == NR - 1:
                            weights_ready((i, j), u + 1)
                        scores((i, j), u + 3)
                        if u < NR - 1:
                            weights_ready((i, j), u + 1)
                        turn_weights((i, j), u + 1)
                        if u < 2 and not beyond(2 * i + j + 1):
                            turn_head(2 * i + j + 1, u)

            with pe.Fori(0, DH // 2 - 1) as i:
                two_heads(i)
            two_heads(DH // 2 - 1)
            for r, (c0, m) in enumerate(RT):
                pe.wait_ge(L["on3_ok"], r + 1)
                if r >= 2:
                    pe.wait_ge(L["on_lo"], NR + r - 1)
                else:
                    pe.wait_ge(L["av_out"], NR * DH + 1)
                for k in range(KT):
                    ins = pe.transpose(ps[:, 2 * (r % 2) + k // 4, (k % 4) * m:(k % 4 + 1) * m], q_r[0:m, r, k * P:(k + 1) * P],
                                       ident[0:m, 0:m])
                ins.then_inc(L["on_turned"], 1)
            pe.wait_ge(L["on_lo"], 2 * NR)
            columns("dout", lambda k: h_parts(h_hi, k), lambda k: h_parts(h_lo, k), squares=3)
            ffn(1)

            pe.wait_ge(tile_read_d, READ_D["end"])
            for r, (c0, m) in enumerate(RT):
                if r >= 2:
                    pe.wait_ge(L["fin_out"], r - 1)
                for k in range(KT):
                    b = 2 * (r % 2) + k // 4
                    ins = pe.transpose(ps[0:m, b, (k % 4) * P:(k % 4 + 1) * P], xT[:, k, c0:c0 + m], ident[:, :])
                ins.then_inc(L["fin_turned"], 1)


        @block.scalar
        def _(act):
            step = Steps(act, act_step)
            A_ = act.activation

            def split(i, j, n0):
                if not (isinstance(i, int) and n0 + 2 * i + j < 2):
                    act.wait_ge(w_used, n0 + 2 * i + j - 1)
                act.wait_ge(w_in[j], 16 * i + 8 * n0 + 16)
                act.copy(w_hi[:, j, :], w_raw[:, j, :]).then_inc(w_hi_ok, 1)

            def next_split(name, i, j):
                split(i + 1 if j else i, 1 - j, BASE[name])

            def rider(name, i, j, half):
                if name in ride:
                    a = 2 * (ride[name] + 2 * i + j) + half
                    act.wait_ge(ada_done, a + 1)
                    act.wait_ge(a_in, 64 * i + 16 * (2 * (ride[name] + j) + half + 1))
                    act.copy(a_hi[:, :], a_raw[:, :]).then_inc(a_hi_ok, 1)

            def over(name, body, last=False):
                pairs = dict(order)[name] // 2
                with act.Fori(0, pairs - last) as i:
                    for j in range(2):
                        rider(name, i, j, 0)
                        next_split(name, i, j)
                        body(i, j, lambda: rider(name, i, j, 1))
                if last:
                    next_split(name, pairs - 1, 0)
                    body(pairs - 1, 0, lambda: None)
                    body(pairs - 1, 1, lambda: None)

            def over_squared(name, which):
                for i in range(dict(order)[name] // 2):
                    for j in range(2):
                        rider(name, i, j, 0)
                        next_split(name, i, j)
                        for t in range(2):
                            m = 4 * i + 2 * j + t
                            if m:
                                act.wait_ge(tile_read_d, READ_D[name] + m)
                                square(which, m - 1)
                            if t == 0:
                                rider(name, i, j, 1)
                act.wait_ge(tile_read_d, READ_D[name] + KT)
                square(which, KT - 1)
                root(which)

            def square(which, k):
                if k >= 2:
                    act.wait_ge(sq_used, which * (KT - 1) + k - 1)
                elif which:
                    act.wait_ge(h_ok, which * KT)
                A_(sq[:, k % 2, :], xT[:, k, :], ACT.Square).then_inc(sq_ok, 1)

            def root(which):
                act.wait_ge(sums_done, which + 1)
                A_(rstd[:, 0:HALF], ps[:, 4, 0:HALF], ACT.Sqrt, bias=eps[:, :], scale=1.0 / D)
                A_(rstd[:, HALF:T], ps[:, 5, 0:HALF], ACT.Sqrt, bias=eps[:, :], scale=1.0 / D).then_inc(root_ok, 1)

            def summed(name, i, j, t):
                if t:
                    act.wait_ge(w_used, BASE[name] + 2 * i + j + 1)
                else:
                    act.wait_ge(tile_done, FIRST[name] + 2 * i + j + 1)

            def row_summed(name, i, j, r):
                if r == NR - 1:
                    act.wait_ge(w_used, BASE[name] + 2 * i + j + 1)
                else:
                    act.wait_ge(rows_done, FIRST_ROWS[name] + (NR - 1) * (2 * i + j) + r + 1)

            act.wait_ge(turned, 1)
            entry = lambda v, m: ps[:, v // 4, (v % 4) * P:(v % 4) * P + m]
            step.then(A_(cs[:, :], entry(0, 2 * KT), ACT.Silu))
            act.copy(norm_g[:, :, :], entry(1, 4 * KT).rearrange("p (l k) -> p l k", k=KT)).then_inc(tile_read_a, 1)
            act.copy(b_ada[:, :, :], entry(2, DEPTH * ADA_TILES).rearrange("p (l k) -> p l k", k=ADA_TILES))
            v = 3
            while v < 3 + 6 * DEPTH:
                e = min(3 + 6 * DEPTH, (v // 4 + 1) * 4)
                src = ps[:, v // 4, (v % 4) * P:(v % 4 + e - v) * P].rearrange("p (v m) -> p v m", m=P)[:, :, 0:2 * FT]
                ins = act.copy(conv_c[:, v - 3:e - 3, :], src)
                v = e
            ins.then_inc(turned_out, 1)
            act.wait_ge(consts, 7)
            act.wait_ge(c_hi_ok, 1)
            act.copy(c_st[:, :, 0:2], cs[:, :].rearrange("p (g k) -> p k g", g=2)).then_inc(c_hi_ok, 1)
            for k in range(KT):
                act.wait_ge(turned, k + 2)
                act.copy(xT[:, k, 0:TP], ps[:, 4 + k % 2, :]).then_inc(x_loaded if k < KT - 2 else rows_free, 1)
            act.copy(xT[:, :, TP:T], ps[:, 6, 0:KT * TS].rearrange("p (k t) -> p k t", t=TS)).then_inc(x_loaded, 1)

            for k in range(KT):
                if k < 2:
                    act.wait_ge(x_loaded, KT - 1)
                square(0, k)
            root(0)
            split(0, 0, 0)
            next_split("ada0", 0, 0)
            next_split("ada0", 0, 1)
            with act.Fori(1, 4) as i:
                next_split("ada0", i, 0)
                next_split("ada0", i, 1)

            def norm(which):
                act.wait_ge(w_used, BASE[AFTER_NORM[which]])
                for k in range(KT):
                    act.wait_ge(xs_ok, which * KT + k + 1)
                    A_(h_hi[:, k, 0:TP], sq[:, k % 2, 0:TP], ACT.Identity, bias=shift[:, k, 0:1])
                    A_(h_hi[:, k, TP:T], sq[:, k % 2, TP:T], ACT.Identity, bias=shift[:, k, 1:2]).then_inc(h_hi_ok, 1)

            norm(0)

            def qk_out(i, j, ride2):
                for t in range(2):
                    if t:
                        ride2()
                    summed("qk", i, j, t)
                    s = (TILE["qk"] + 2 * j + t) % 2
                    m = 4 * i + 2 * j + t
                    act.copy(qk[:, bass.ds(m, 1), 0:HALF], ps[:, 2 * s, None, 0:HALF])
                    act.copy(qk[:, bass.ds(m, 1), HALF:T], ps[:, 2 * s + 1, None, 0:HALF]).then_inc(tile_read_a, 1)

            over("qk", qk_out)
            act.wait_ge(phase_in, 64)
            act.copy(aw_hi[:, :, :], aw[:, :, :]).then_inc(L["aw_hi_ok"], 1)
            act.wait_ge(tile_done, FIRST["alow"] + 1)
            t = TILE["alow"]
            act.wait_ge(L["al_ok"], 1)
            act.copy(alT[0:RANK, 0:HALF], slot(t, 0, m=RANK))
            act.copy(alT[0:RANK, HALF:T], slot(t, 1, m=RANK)).then_inc(tile_read_a, 1)

            def rows_out(name, dst, func):
                def body(i, j, ride2):
                    for r, (c0, m) in enumerate(RT):
                        if r == 2:
                            ride2()
                        row_summed(name, i, j, r)
                        A_(dst[0:m, r, bass.ds((2 * i + j) * BLOCK_COLS, BLOCK_COLS)], ps[0:m, 4 + (NR * j + r) % 2, 0:BLOCK_COLS],
                           func).then_inc(rows_free, 1)
                over(name, body)

            rows_out("v", v_r, ACT.Copy)
            rows_out("r", r_r, ACT.Silu)

            def gates(r):
                if r >= NR:
                    return
                m = RT[r][1]
                act.wait_ge(L["logit_ok"], r + 1)
                if r:
                    act.wait_ge(L["attn_ok"], r)
                A_(tB[0:m, :], ps[0:m, 7, :], ACT.Abs).then_inc(L["logit_out"], 1)
                act.wait_ge(L["logit_out"], r + 1)
                step.then(A_(tB[0:m, :], tB[0:m, :], ACT.Exp, scale=-1.0))
                A_(tB[0:m, :], tB[0:m, :], ACT.Ln, bias=1.0).then_inc(L["lsp_ok"], 1)

            def decays(r):
                if r >= NR:
                    return
                m = RT[r][1]
                nch = max(1, m // CHUNK)
                n = GH * m
                act.wait_ge(L["bd_ok"], r + 1)
                if r >= 2:
                    act.wait_ge(L["o_ok"], r - 1)
                last = tA[:, 0:n].rearrange("p (h c t) -> p h c t", h=GH, c=nch)[:, :, :, m // nch - 1]
                A_(dec[:, :, 0:nch], last, ACT.Exp)
                A_(qe[r % 2][:, 0:n], tA[:, 0:n], ACT.Exp)
                A_(tB[:, 0:n], tA[:, 0:n], ACT.Exp, scale=-1.0)
                A_(tC[:, 0:n], tC[:, 0:n], ACT.Exp, scale=-1.0).then_inc(L["exp_ok"], 1)

            def keys_out(r):
                if r < NR:
                    m = RT[r][1]
                    act.wait_ge(L["kd_turned"], r + 1)
                    if r >= 2:
                        act.wait_ge(L["u_ok"], r - 1)
                    act.copy(kd_r[r % 2][0:m, :], ps[0:m, 0, :]).then_inc(L["kd_out"], 1)

            gates(0)
            decays(0)
            keys_out(0)
            for r, (c0, m) in enumerate(RT):
                gates(r + 1)
                decays(r + 1)
                act.wait_ge(L["o_ok"], r + 1)
                for h in range(GH):
                    ins = A_([qe, kd_r][h // 2][r % 2][0:m, (h % 2) * DV:(h % 2 + 1) * DV],
                             ps[0:m, [4, 6][h // 2], (h % 2) * DV:(h % 2 + 1) * DV], ACT.Square, accum_out=stat[0:m, h:h + 1])
                step.then(ins)
                A_(stat[0:m, 4:4 + GH], stat[0:m, 0:GH], ACT.Sqrt, bias=eps[0:m, :], scale=1.0 / DV).then_inc(L["oss_ok"], 1)
                keys_out(r + 1)
                act.wait_ge(L["on_turned"], r + 1)
                if r == 0:
                    act.wait_ge(w_used, BASE["gout"])
                for b in range(2):
                    ins = act.copy(h_hi[:, 4 * b:4 * b + 4, c0:c0 + m], ps[:, [4, 6][b], 0:4 * m].rearrange("p (k t) -> p k t", k=4))
                ins.then_inc(L["on_hi"], 1)
            over_squared("gout", 1)

            def ffn(l):
                norm(2 * l + 1)
                if l:
                    act.wait_ge(L["nc_turned"], l)
                else:
                    act.wait_ge(state_out, 32)
                done = {"up": 0}
                for kind, c in ffn_order:
                    name = (l, kind, c)
                    last = l == DEPTH - 1 and (kind, c) == ffn_order[-1]
                    if name == BEFORE_NORM[2]:
                        over_squared(name, 2)
                        continue
                    if kind == "down":
                        over(name, lambda i, j, ride2: ride2(), last=last)
                        continue
                    c0 = sum(CH[:c])
                    u0 = 2 * c0
                    if c >= 2:
                        act.wait_ge(w_used, BASE[(l, "down", c - 2)] + nblk("down", c - 2))

                    def body(i, j, ride2):
                        for t in range(2):
                            if t:
                                ride2()
                            u = u0 + 4 * i + 2 * j + t
                            summed(name, i, j, t)
                            act.wait_ge(conv_ok, l * (2 * FT * 1 + 2) + u + 1)
                            s = (TILE[name] + 2 * j + t) % 2
                            ft = j * FT + c0 + 2 * i + t
                            act.copy(up[:, t, 2:2 + HALF], ps[:, 2 * s, 0:HALF])
                            act.copy(up[:, t, 2 + HALF:2 + TP], ps[:, 2 * s + 1, 0:PB])
                            act.copy(up[:, t, TP + 4:T + 4], ps[:, 2 * s + 1, PB:HALF])
                            act.copy(up[:, t, TP + 2:TP + 4], conv_c[:, 6 * l + 4:6 * l + 6, bass.ds(ft, 1)].rearrange("p a b -> p (a b)"))
                            ends = ps[:, 2 * s + 1, PB - 2:PB - 2 + 2 * TS].rearrange("p (g t) -> p g t", g=2)[:, :, 0:2]
                            act.copy(new_conv[:, bass.ds(ft, 1), :].rearrange("p a (g t) -> p (a g) t", g=2), ends).then_inc(tile_read_a, 1)
                            act.wait_ge(tile_read_a, READ_A[name] + 4 * i + 2 * j + t + 1)
                            A_(cv1[:, t, :], up[:, t, 0:W], ACT.Identity, scale=conv_c[:, 6 * l, bass.ds(ft, 1)],
                               bias=conv_c[:, 6 * l + 3, bass.ds(ft, 1)]).then_inc(up_ok, 1)
                            if j:
                                pr_n = l * FT + c0 + 2 * i + t
                                act.wait_ge(conv_ok, l * (2 * FT + 2) + u + 3)
                                A_(cv[:, 1, t, :], cv[:, 1, t, :], ACT.Silu).then_inc(silu_ok, 1)
                                act.wait_ge(prod_ok, pr_n + 1)
                                act.copy(act_hi[:, c % 2, bass.ds(2 * i + t, 1), :], cv[:, 0, t, None, :]).then_inc(act_hi_ok, 1)
                    over(name, body)

            ffn(0)

            norm(2)

            def qkv_out(name, dst, which):
                def body(i, j, ride2):
                    for r, (c0, m) in enumerate(RT):
                        if r == 2:
                            ride2()
                        row_summed(name, i, j, r)
                        src = ps[0:m, 4 + (NR * j + r) % 2, 0:BLOCK_COLS]
                        if which < 2:
                            k = which * 4 * NR + 2 * NR * i + NR * j + r
                            act.wait_ge(L["ssq_used"], k + 1)
                            b = (NR * j + r) % 2
                            A_(ssq[0:m, b * BLOCK_COLS:(b + 1) * BLOCK_COLS], src, ACT.Square).then_inc(L["ssq_ok"], 1)
                        A_(dst[0:m, r, bass.ds((2 * i + j) * BLOCK_COLS, BLOCK_COLS)], src, ACT.Copy).then_inc(rows_free, 1)
                over(name, body)

            qkv_out("dq", q_r, 0)
            qkv_out("dk", k_r, 1)
            act.wait_ge(L["ssq_used"], 2 + 8 * NR)
            A_(rs[:, :, :, :], ss[:, :, :, :], ACT.Sqrt, bias=eps[:, :], scale=1.0 / HD).then_inc(L["rs_ok"], 1)
            qkv_out("dv", vd_r, 2)
            act.wait_ge(L["lam_ok"], 1)
            A_(stat[:, 34:36], stat[:, 32:34], ACT.Exp).then_inc(L["lam_ok"], 1)
            act.sem_inc(L["av_out"], 1)

            def head_out(h, hp, part):
                act.wait_ge(L["head_turned"], 2 * h + part + 1)
                dst = qT[hp][:, 0:TP] if part == 0 else kcT[hp][:, 0:PAST]
                act.copy(dst, ps[:, 2, :]).then_inc(L["head_outA"], 1)

            def exps(at, ahead):
                h, u, n, s = unit(at, ahead)
                if beyond(h):
                    return
                r = UNITS[u]
                m = RT[r][1]
                if not (isinstance(n, int) and n < 2):
                    act.wait_ge(L["a_turned"], n - 1)
                act.wait_ge(L["mx_ok"], n + 1)
                s0 = 8 * s
                for c in range(2):
                    nk = (r + 1) * P if r < NPR else PAST
                    ins = A_(pr[0:m, s, c, 0:nk], ps[0:m, 4 + 2 * s + c, 0:nk], ACT.Exp, bias=stat[0:m, s0 + c:s0 + c + 1],
                             accum_out=stat[0:m, s0 + 2 + c:s0 + 3 + c])
                    if r == NPR:
                        ins = A_(pr[0:m, s, c, PAST:PAST + TS], ps[0:m, 2 + c, 0:TS], ACT.Exp,
                                 bias=stat[0:m, s0 + c:s0 + c + 1], accum_out=stat[0:m, s0 + 4 + c:s0 + 5 + c])
                ins.then_inc(L["p_ok"], 1)

            def weights_out(at, ahead):
                h, u, n, s = unit(at, ahead)
                if beyond(h):
                    return
                r = UNITS[u]
                m = RT[r][1]
                nb = r + 1 if r < NPR else NPAST
                act.wait_ge(L["a_turned"], n + 1)
                if not (isinstance(n, int) and n < 1):
                    act.wait_ge(L["av_ok"], n)
                ins = act.copy(aT[:, 0:nb * m], ps[:, 0, 0:nb * m])
                if r == NPR:
                    ins = act.copy(aT[0:TS, nb * m:(nb + 1) * m], ps[0:TS, 0, nb * m:(nb + 1) * m])
                ins.then_inc(L["a_out"], 1)

            def values_out(at, ahead):
                h, u, n, s = unit(at, ahead)
                r = UNITS[u]
                m = RT[r][1]
                inv = stat[0:m, 40 + 2 * u:41 + 2 * u]
                act.wait_ge(L["av_ok"], n + 1)
                A_(q_r[0:m, r, bass.ds(h * EV, EV)], ps[0:m, 1, 0:EV], ACT.Identity, scale=inv)
                A_(osq[0:m, :], ps[0:m, 1, 0:EV], ACT.Square, scale=inv, accum_out=oss[0:m, r, bass.ds(h, 1)]).then_inc(L["av_out"], 1)

            head_out(0, 0, 0)
            head_out(0, 0, 1)
            exps((0, 0), 0)
            exps((0, 0), 1)
            weights_out((0, 0), 0)
            def two_heads(i):
                for j in range(2):
                    for u in range(NR):
                        exps((i, j), u + 2)
                        values_out((i, j), u)
                        weights_out((i, j), u + 1)
                        if u < 2 and not beyond(2 * i + j + 1):
                            head_out(2 * i + j + 1, (j + 1) % 2, u)

            with act.Fori(0, DH // 2 - 1) as i:
                two_heads(i)
            two_heads(DH // 2 - 1)
            act.wait_ge(L["av_out"], NR * DH + 1)
            A_(ors[:, :, :], oss[:, :, :], ACT.Sqrt, bias=eps[:, :], scale=1.0 / EV).then_inc(L["osq_ok"], 1)
            for r, (c0, m) in enumerate(RT):
                act.wait_ge(L["on_turned"], NR + r + 1)
                for b in range(2):
                    ins = A_(h_hi[:, 4 * b:4 * b + 4, c0:c0 + m], ps[:, 2 * (r % 2) + b, 0:4 * m].rearrange("p (k t) -> p k t", k=4),
                             ACT.Identity, scale=d_gain[:, :])
                ins.then_inc(L["on_hi"], 1)
            over_squared("dout", 3)
            ffn(1)
            for r, (c0, m) in enumerate(RT):
                act.wait_ge(L["fin_turned"], r + 1)
                if r >= 2:
                    act.wait_ge(L["fin_stored%d" % (r % 2)], 16 * (r // 2))
                for b in range(2):
                    ins = act.copy(y_rows[0:m, r % 2, b * 512:(b + 1) * 512], ps[0:m, 2 * (r % 2) + b, :])
                ins.then_inc(L["fin_out"], 1)

        @block.vector
        def _(dve):
            step = Steps(dve, dve_step)
            TT, STT = dve.tensor_tensor, dve.scalar_tensor_tensor
            f32 = lambda ap: ap.bitcast(F32)

            def split(i, j, n0):
                dve.wait_ge(w_hi_ok, n0 + 2 * i + j + 1)
                TT(w_lo[:, j, :], w_raw[:, j, :], f32(w_hi[:, j, :]), ALU.subtract).then_inc(w_lo_ok, 1)

            def next_split(name, i, j):
                split(i + 1 if j else i, 1 - j, BASE[name])

            def ada_out(l, b):
                dve.transpose(ada_t[:, :], ps[0:32, 7, 0:BLOCK_COLS]).then_inc(ada_free, 1)

            def ada_sum(l, b, done):
                dve.wait_ge(ada_free, done)
                v = ada_t[:, :].rearrange("p (t q c) -> p t q c", t=2, q=4)
                for q in range(4):
                    ins = TT(ada[32 * q:32 * q + 32, l, bass.ds(2 * b, 2), :], v[:, :, q, 0:2], v[:, :, q, 2:4], ALU.add)
                step.then(ins)

            def over(name, body, last=False, per=0):
                pairs = dict(order)[name] // 2
                riding = name in ride
                with dve.Fori(0, pairs - last) as i:
                    step.loop(i, per + 2 * riding)
                    for j in range(2):
                        def rider(half):
                            if riding:
                                dve.wait_ge(a_hi_ok, 2 * (ride[name] + 2 * i + j) + half + 1)
                                TT(a_lo[:, :], a_raw[:, :], f32(a_hi[:, :]), ALU.subtract).then_inc(a_lo_ok, 1)

                        rider(0)
                        next_split(name, i, j)
                        body(i, j, lambda: rider(1))
                        if riding:
                            a = ride[name] + 2 * i + j
                            l, b0 = shared_ride(name)
                            dve.wait_ge(ada_done, 2 * a + 3)
                            ada_out(l, b0 + 2 * i + j)
                            ada_sum(l, b0 + 2 * i + j, a + 9)
                step.end(pairs - last)
                if last:
                    next_split(name, pairs - 1, 0)
                    body(pairs - 1, 0, lambda: None)
                    body(pairs - 1, 1, lambda: None)

            dve.memset(c_st[:, :, :].bitcast(F32), 0.0).then_inc(c_hi_ok, 1)
            dve.wait_ge(c_hi_ok, 2)
            TT(c_st[:, :, 2:4], cs[:, :].rearrange("p (g k) -> p k g", g=2), f32(c_st[:, :, 0:2]), ALU.subtract).then_inc(c_st_ok, 1)
            split(0, 0, 0)

            def ada_main(i):
                for j in range(2):
                    next_split("ada0", i, j)
                    dve.wait_ge(w_used, 2 * i + j + 1)
                    ada_out(0, 2 * i + j)
                    ada_sum(0, 2 * i + j, 2 * i + j + 1)

            ada_main(0)
            dve.wait_ge(root_ok, 1)
            dve.reciprocal(rstd[:, :], rstd[:, :]).then_inc(rms_used, 1)
            with dve.Fori(1, 4) as i:
                step.at, step.n, before_loop = (i - 1) * 2 + step.n, 0, step.n
                ada_main(i)
            step.at, step.n = before_loop + 6, 0

            def add_bias(dst, l, first):
                b = b_ada[:, l, first * KT:(first + 1) * KT, None].broadcast_to([P, KT, 2])
                step.then(TT(dst[:, :, :], ada[:, l, first * KT:(first + 1) * KT, :], b, ALU.add))

            def invert(which):
                dve.wait_ge(root_ok, which + 1)
                dve.reciprocal(rstd[:, :], rstd[:, :]).then_inc(rms_used, 1)

            def norm(which):
                l, sub = which // 2, which % 2
                add_bias(shift, l, 3 * sub)
                add_bias(gain, l, 3 * sub + 1)
                ng = norm_g[:, 2 * sub + l, :, None].broadcast_to([P, KT, 2])
                step.then(STT(out=gain[:, :, :], in0=gain[:, :, :], scalar=1.0, in1=ng, op0=ALU.add, op1=ALU.mult))
                if which:
                    invert(which)
                dve.wait_ge(rms_used, which + 1)

                def scaled(k):
                    for gq, c in ((0, slice(0, TP)), (1, slice(TP, T))):
                        ins = STT(out=sq[:, k % 2, c], in0=xT[:, k, c], scalar=gain[:, k, gq:gq + 1], in1=rstd[:, c],
                                  op0=ALU.mult, op1=ALU.mult)
                    ins.then_inc(xs_ok, 1)

                scaled(0)
                for k in range(KT):
                    if k + 1 < KT:
                        if k:
                            dve.wait_ge(h_ok, which * KT + k)
                        scaled(k + 1)
                    dve.wait_ge(h_hi_ok, which * KT + k + 1)
                    for gq, c in ((0, slice(0, TP)), (1, slice(TP, T))):
                        ins = STT(out=h_lo[:, k, c], in0=sq[:, k % 2, c], scalar=shift[:, k, gq:gq + 1], in1=f32(h_hi[:, k, c]),
                                  op0=ALU.add, op1=ALU.subtract)
                    ins.then_inc(h_ok, 1)

            def stream_out(name, junk):
                def body(i, j, ride2):
                    for t in range(2):
                        if t:
                            ride2()
                            dve.wait_ge(w_used, BASE[name] + 2 * i + j + 1)
                        else:
                            dve.wait_ge(tile_done, FIRST[name] + 2 * i + j + 1)
                        dve.wait_ge(tile_read_d, READ_D[name] + 4 * i + 2 * j + t)
                        s = (TILE[name] + 2 * j + t) % 2
                        m = 4 * i + 2 * j + t
                        for gq, c, b, c1 in ((0, slice(0, HALF), 0, 0), (0, slice(HALF, TP), 1, 0), (1, slice(TP, T), 1, PB + junk)):
                            x = xT[:, bass.ds(m, 1), c].rearrange("p a t -> p (a t)")
                            ins = STT(out=x, in0=ps[:, 2 * s + b, c1:c1 + c.stop - c.start],
                                      scalar=gate[:, bass.ds(m, 1), gq:gq + 1].rearrange("p a t -> p (a t)"), in1=x,
                                      op0=ALU.mult, op1=ALU.add)
                        ins.then_inc(tile_read_d, 1)
                return body

            norm(0)
            over("qk", lambda i, j, ride2: ride2())
            dve.wait_ge(L["aw_hi_ok"], 1)
            dve.memset(alT[:, :], 1.0).then_inc(L["al_ok"], 1)
            TT(aw_lo[:, :, :], aw[:, :, :], f32(aw_hi[:, :, :]), ALU.subtract).then_inc(L["aw_ok"], 1)
            over("v", lambda i, j, ride2: ride2())
            over("r", lambda i, j, ride2: ride2())
            dve.wait_ge(w_used, BASE["gout"])
            dve.memset(att[0][:, :], 0.0)
            dve.memset(att[1][:, :], 0.0)
            dve.memset(S[:, 0, :, :], 0.0).then_inc(L["s_zero"], 1)

            def gates(r):
                if r >= NR:
                    return
                m = RT[r][1]
                rg = r_r[0:m, r, :].rearrange("p (h e) -> p h e", h=GH)
                if r == 0:
                    dve.wait_ge(rows_free, ROWS["dq"] + 2)
                TT(rg, rg, gla_g[0:m, None, :].broadcast_to([m, GH, DV]), ALU.mult).then_inc(L["dg_ok"], 1)
                dve.wait_ge(L["logit_out"], r + 1)
                step.then(dve.tensor_scalar(tA[0:m, :], ps[0:m, 7, :], 0.0, None, ALU.min))
                dve.wait_ge(L["lsp_ok"], r + 1)
                TT(tA[0:m, :], tA[0:m, :], tB[0:m, :], ALU.subtract).then_inc(L["g_ok"], 1)

            def decayed(r):
                if r >= NR:
                    return
                c0, m = RT[r]
                nch = max(1, m // CHUNK)
                C = m // nch
                n = GH * m
                hm = lambda t: t[:, 0:n].rearrange("p (h t) -> p h t", h=GH)
                dve.wait_ge(L["b_ok"], r + 1)
                dve.tensor_copy(tA[:, 0:n], ps[:, 7, 0:n]).then_inc(L["b_sb_ok"], 1)
                dve.wait_ge(L["b_sb_ok"], r + 1)
                hc = lambda t: t[:, 0:n].rearrange("p (h t) -> p h t", t=C)
                TT(hc(tC), hc(tA), hc(tA)[:, :, C - 1:C].broadcast_to([P, GH * nch, C]), ALU.subtract).then_inc(L["bd_ok"], 1)
                dve.wait_ge(L["exp_ok"], r + 1)
                q, k = qk[:, 0:GH, c0:c0 + m], qk[:, GH:2 * GH, c0:c0 + m]
                STT(out=hm(qe[r % 2]), in0=q, scalar=DK ** -0.5, in1=hm(qe[r % 2]), op0=ALU.mult, op1=ALU.mult)
                TT(hm(tB), k, hm(tB), ALU.mult)
                TT(hm(tC), k, hm(tC), ALU.mult).then_inc(L["qe_ok"], 1)

            def scores_out(r):
                if r >= NR:
                    return
                m = RT[r][1]
                n = GH * m
                dve.wait_ge(L["attn_ok"], r + 1)
                if r == NPR:
                    step.then(dve.memset(att[r % 2][:, :], 0.0))
                if r == 0:
                    dve.wait_ge(L["s_zero"], 1)
                    dve.wait_ge(consts, 7)
                dve.copy_predicated(att[r % 2][0:m, 0:n].rearrange("p (h t) -> p h t", h=GH),
                                    cum[0:m, None, 0:m].broadcast_to([m, GH, m]).bitcast(U32),
                                    ps[0:m, 7, 0:n].rearrange("p (h t) -> p h t", h=GH)).then_inc(L["attn_out"], 1)

            gates(0)
            decayed(0)
            scores_out(0)
            for r, (c0, m) in enumerate(RT):
                nch = max(1, m // CHUNK)
                gates(r + 1)
                dve.wait_ge(L["u_ok"], r + 1)
                s0 = 2 * r if r < NPR else 2 * NPR + 1
                if r == NPR:
                    dve.wait_ge(L["s_in"], 16)
                for c in range(nch):
                    for h in range(GH):
                        b = [[1, 2], [3, 5]][c][h // 2]
                        ins = STT(out=S[:, (s0 + c + 1) % 3, h, :], in0=S[:, (s0 + c) % 3, h, :], scalar=dec[:, h, c:c + 1],
                                  in1=ps[:, b, (h % 2) * DV:(h % 2 + 1) * DV], op0=ALU.mult, op1=ALU.add)
                        if nch == 1 and h == GH - 2 or nch > 1 and c == 0 and h == GH - 1:
                            ins.then_inc(L["s1_ok"], 1)
                            if nch > 1:
                                dve.wait_ge(L["s1_ok"], r + 1)
                ins.then_inc(L["s2_ok"], 1)
                decayed(r + 1)
                dve.wait_ge(L["oss_ok"], r + 1)
                step.then(dve.reciprocal(stat[0:m, 8:8 + GH], stat[0:m, 4:4 + GH]))
                for h in range(GH):
                    ins = STT(out=r_r[0:m, r, h * DV:(h + 1) * DV], in0=ps[0:m, [4, 6][h // 2], (h % 2) * DV:(h % 2 + 1) * DV],
                              scalar=stat[0:m, 8 + h:9 + h], in1=r_r[0:m, r, h * DV:(h + 1) * DV], op0=ALU.mult, op1=ALU.mult)
                ins.then_inc(L["on_ok"], 1)
                scores_out(r + 1)
                dve.wait_ge(L["on_hi"], r + 1)
                for b in range(2):
                    k4 = slice(4 * b, 4 * b + 4)
                    ins = TT(h_lo[:, k4, c0:c0 + m], ps[:, [4, 6][b], 0:4 * m].rearrange("p (k t) -> p k t", k=4), f32(h_hi[:, k4, c0:c0 + m]),
                             ALU.subtract)
                    if r >= NR - 2 and b == 0:
                        ins.then_inc(tile_read_d, 1)
                ins.then_inc(L["on_lo"], 1)
            add_bias(gate, 0, 2)
            over("gout", stream_out("gout", 0))

            def ffn(l):
                norm(2 * l + 1)
                add_bias(gate, l, 5)
                dve.wait_ge(w_used, BASE[(l, "up", 0)])
                if l == 0:
                    dve.wait_ge(state_out, 32)
                for t in range(2):
                    dve.memset(up[:, t, 0:2], 0.0).then_inc(conv_ok, 1)
                for kind, c in ffn_order:
                    name = (l, kind, c)
                    last = l == DEPTH - 1 and (kind, c) == ffn_order[-1]
                    if kind == "down":
                        over(name, stream_out(name, 2), last=last)
                        continue
                    c0 = sum(CH[:c])

                    def body(i, j, ride2):
                        for t in range(2):
                            if t:
                                ride2()
                            ft = j * FT + c0 + 2 * i + t
                            dve.wait_ge(up_ok, l * 2 * FT + 2 * c0 + 4 * i + 2 * j + t + 1)
                            w = lambda n: conv_c[:, 6 * l + n, bass.ds(ft, 1)]
                            step.then(STT(out=cv1[:, t, :], in0=up[:, t, 1:W + 1], scalar=w(1), in1=cv1[:, t, :], op0=ALU.mult, op1=ALU.add))
                            STT(out=cv[:, j, t, :], in0=up[:, t, 2:W + 2], scalar=w(2), in1=cv1[:, t, :], op0=ALU.mult,
                                op1=ALU.add).then_inc(conv_ok, 1)
                            if j:
                                n = l * FT + c0 + 2 * i + t
                                dve.wait_ge(silu_ok, n + 1)
                                TT(cv[:, 0, t, :], cv[:, 1, t, :], cv[:, 0, t, :], ALU.mult).then_inc(prod_ok, 1)
                                dve.wait_ge(act_hi_ok, n + 1)
                                m1 = bass.ds(2 * i + t, 1)
                                TT(act_lo[:, c % 2, m1, :], cv[:, 0, t, None, :], f32(act_hi[:, c % 2, m1, :]), ALU.subtract).then_inc(act_ok, 1)
                    over(name, body, per=4)
                dve.wait_ge(L["nc_turned"], l + 1)
                if l:
                    dve.wait_ge(L["nc_stored"], 64 * l)
                dve.tensor_copy(nc_rows[:, :, :], ps[0:2 * FT, 6, :].rearrange("p (g t) -> p g t", g=4)).then_inc(L["nc_out"], 1)

            ffn(0)

            dve.wait_ge(act_ok, FT)
            dve.memset(q_r[:, NPR, :], 1.0).then_inc(L["ssq_used"], 1)
            dve.memset(k_r[:, NPR, :], 1.0).then_inc(L["ssq_used"], 1)
            dve.memset(oss[:, :, :], 1.0)
            step.then(dve.memset(ss[:, :, :, :], 1.0))
            norm(2)

            def sums(name, which):
                def body(i, j, ride2):
                    for r, (c0, m) in enumerate(RT):
                        k = which * 4 * NR + 2 * NR * i + NR * j + r
                        b = (NR * j + r) % 2
                        if r == 2:
                            ride2()
                        dve.wait_ge(L["ssq_ok"], k + 1)
                        dve.tensor_reduce(ss[0:m, r, which, bass.ds(4 * (2 * i + j), 4)],
                                          ssq[0:m, b * BLOCK_COLS:(b + 1) * BLOCK_COLS].rearrange("p (g d) -> p g d", d=HD),
                                          AX_X, ALU.add).then_inc(L["ssq_used"], 1)
                over(name, body)

            sums("dq", 0)
            sums("dk", 1)
            dve.wait_ge(L["rs_ok"], 1)
            step.then(dve.reciprocal(ss[:, :, :, :], rs[:, :, :, :]))
            over("dv", lambda i, j, ride2: ride2())
            dve.wait_ge(phase_in, 128)
            lp = lam_in[:, :, :].rearrange("p (a b) d -> p a b d", b=2)
            step.then(TT(lp[:, :, 0, :], lp[:, :, 0, :], lp[:, :, 1, :], ALU.mult))
            dve.tensor_reduce(stat[:, 32:34], lp[:, :, 0, :], AX_X, ALU.add).then_inc(L["lam_ok"], 1)
            dve.wait_ge(L["lam_ok"], 2)
            step.then(TT(stat[:, 36:37], stat[:, 35:36], stat[:, 34:35], ALU.subtract))
            step.then(dve.tensor_scalar(stat[:, 37:38], stat[:, 36:37], -LAM_INIT, None, ALU.add))
            step.then(dve.tensor_scalar(d_gain[:, :], d_gain[:, :], 1.0 - LAM_INIT, None, ALU.mult))
            step.then(dve.tensor_scalar(q_gain[:, :], q_gain[:, :], SCALE, None, ALU.mult))

            def normalise(h):
                if not (isinstance(h, int) and h == 0):
                    dve.wait_ge(L["head_turned"], 2 * h)
                    dve.wait_ge(L["kn_out"], 32 * h)
                for w, (src, dst) in enumerate(((q_r, qn), (k_r, kn))):
                    x = src[:, :, bass.ds(h * EV, EV)].rearrange("p r (s d) -> p r s d", d=HD)
                    rr = ss[:, :, w, bass.ds(2 * h, 2)][:, :, :, None].broadcast_to([P, NR, 2, HD])
                    ins = TT(dst[:, :, :].rearrange("p r (s d) -> p r s d", d=HD), x, rr, ALU.mult)
                ins.then_inc(L["qn_ok"], 1)

            def head_out(h, hp, part):
                dve.wait_ge(L["head_turned"], 2 * h + part + 1)
                if part == 0:
                    ins = dve.tensor_copy(kT[hp][:, 0:TP], ps[:, 3, :])
                else:
                    dve.tensor_copy(qT[hp][:, TP:T], ps[:, 3, 0:TS])
                    ins = dve.tensor_copy(kT[hp][:, TP:T], ps[:, 3, TS:2 * TS])
                ins.then_inc(L["head_outD"], 1)

            def maxima(at, ahead):
                h, u, n, s = unit(at, ahead)
                if beyond(h):
                    return
                r = UNITS[u]
                m = RT[r][1]
                out = stat[0:m, 8 * s:8 * s + 2]
                b = 4 + 2 * s
                dve.wait_ge(L["sc_ok"], n + 1)
                if r < NPR:
                    ins = dve.tensor_reduce(out, ps[0:m, b:b + 2, 0:(r + 1) * P], AX_X, ALU.max, negate=True)
                else:
                    dve.tensor_reduce(stat[0:m, 16:18], ps[0:m, b:b + 2, 0:PAST], AX_X, ALU.max, negate=True)
                    step.then(dve.tensor_reduce(stat[0:m, 18:20], ps[0:m, 2:4, 0:TS], AX_X, ALU.max, negate=True))
                    ins = TT(out, stat[0:m, 16:18], stat[0:m, 18:20], ALU.min)
                ins.then_inc(L["mx_ok"], 1)

            def weights(at, ahead):
                h, u, n, s = unit(at, ahead)
                if beyond(h):
                    return
                r = UNITS[u]
                m = RT[r][1]
                s0 = 8 * s
                nk = (r + 1) * P if r < NPR else PAST + TS
                dve.wait_ge(L["p_ok"], n + 1)
                den, inv = stat[0:m, s0 + 2:s0 + 4], stat[0:m, 40 + 2 * u:42 + 2 * u]
                if r == NPR:
                    step.then(TT(den, den, stat[0:m, s0 + 4:s0 + 6], ALU.add))
                step.then(dve.reciprocal(inv, den))
                step.then(STT(out=stat[0:m, s0 + 6:s0 + 7], in0=inv[:, 1:2], scalar=den[:, 0:1], in1=stat[0:m, 37:38], op0=ALU.mult, op1=ALU.mult))
                STT(out=pr[0:m, s, 0, 0:nk], in0=pr[0:m, s, 1, 0:nk], scalar=stat[0:m, s0 + 6:s0 + 7], in1=pr[0:m, s, 0, 0:nk],
                    op0=ALU.mult, op1=ALU.add).then_inc(L["a_ok"], 1)

            normalise(0)
            head_out(0, 0, 0)
            head_out(0, 0, 1)
            maxima((0, 0), 0)
            maxima((0, 0), 1)
            weights((0, 0), 0)
            maxima((0, 0), 2)
            normalise(1)
            def two_heads(i):
                looped = not isinstance(i, int)
                if looped:
                    step.loop(i, 2 * (2 * NR + 2))
                for j in range(2):
                    for u in range(NR):
                        weights((i, j), u + 1)
                        maxima((i, j), u + 3)
                        if u < 2 and not beyond(2 * i + j + 1):
                            head_out(2 * i + j + 1, (j + 1) % 2, u)
                        if u == 3 and not beyond(2 * i + j + 2):
                            normalise(2 * i + j + 2)
                if looped:
                    step.end(DH // 2 - 1)

            with dve.Fori(0, DH // 2 - 1) as i:
                two_heads(i)
            two_heads(DH // 2 - 1)
            dve.wait_ge(L["osq_ok"], 1)
            step.then(dve.reciprocal(oss[:, :, :], ors[:, :, :]))

            def output_rows(r):
                m = RT[r][1]
                o = q_r[0:m, r, :].rearrange("p (h e) -> p h e", h=DH)
                TT(o, o, oss[0:m, r, :, None].broadcast_to([m, DH, EV]), ALU.mult).then_inc(L["on3_ok"], 1)

            output_rows(0)
            for r, (c0, m) in enumerate(RT):
                if r + 1 < NR:
                    output_rows(r + 1)
                dve.wait_ge(L["on_hi"], NR + r + 1)
                for b in range(2):
                    k4 = slice(4 * b, 4 * b + 4)
                    ins = STT(out=h_lo[:, k4, c0:c0 + m], in0=ps[:, 2 * (r % 2) + b, 0:4 * m].rearrange("p (k t) -> p k t", k=4),
                              scalar=d_gain[:, :], in1=f32(h_hi[:, k4, c0:c0 + m]), op0=ALU.mult, op1=ALU.subtract)
                ins.then_inc(L["on_lo"], 1)
            add_bias(gate, 1, 2)
            over("dout", stream_out("dout", 0))
            ffn(1)


_INS = ['x_prompt', 'x_sample', 'state_gla', 'cache_diff_k', 'cache_diff_v', 'state_ffn_conv', 'c_prompt', 'c_sample',
        'norm_mix', 'norm_ffn', 'w_ada', 'b_ada', 'gla_w_in', 'gla_w_alpha', 'gla_b_alpha', 'gla_norm', 'gla_w_out',
        'diff_w_in', 'diff_q_norm', 'diff_k_norm', 'diff_lambda', 'diff_norm', 'diff_w_out',
        'ffn_w_in', 'ffn_conv_w', 'ffn_conv_b', 'ffn_w_out']


def kernel(**inputs):
    import numpy as np
    from concourse import bacc
    from concourse.bass_utils import run_bass_kernel_spmd

    nc = bacc.Bacc("TRN2", target_bir_lowering=False, num_devices=1)
    arrays, aps = {}, {}
    for name in _INS:
        a = np.ascontiguousarray(inputs[name])
        arrays[f"in_{name}"] = a
        aps[name] = nc.dram_tensor(f"in_{name}", a.shape, mybir.dt.from_np(a.dtype), kind="ExternalInput").ap()
    xp, xs = inputs["x_prompt"].shape, inputs["x_sample"].shape
    sg, ck, cv = inputs["state_gla"].shape, inputs["cache_diff_k"].shape, inputs["cache_diff_v"].shape
    fc = inputs["state_ffn_conv"].shape
    shapes = [xp, xs, (sg[0], xp[0]) + sg[2:], sg,
              (ck[0], xp[0], xp[1]) + ck[3:], (ck[0], xs[0], xs[1]) + ck[3:],
              (cv[0], xp[0], xp[1]) + cv[3:], (cv[0], xs[0], xs[1]) + cv[3:],
              (fc[0], xp[0]) + fc[2:], fc]
    outs = [nc.dram_tensor(f"out_{i}", s, F32, kind="ExternalOutput").ap() for i, s in enumerate(shapes)]
    hybrid_stream_step(nc, aps, outs)
    r = run_bass_kernel_spmd(nc, [arrays], core_ids=[0])
    return tuple(r.results[0][f"out_{i}"] for i in range(len(shapes)))
```
